# Optimizing a Trainium2 kernel written in Bass

```python
import math
import jax
import jax.numpy as jnp
from jax import lax
import numpy as np
import jax, jax.numpy as jnp

D_MODEL = 2048
BATCH = 1
SEQ = 256
DEPTH = 1

N_MIXERS = 2
N_META = 16
CONV_WIDTH = 31
HEAD_DIM = 64
N_HEADS = D_MODEL // HEAD_DIM
N_KV_HEADS = N_HEADS // 8
GROUP = N_HEADS // N_KV_HEADS
WINDOW = 128
BLOCK = 128
N_BUCKETS = 32
MAX_DISTANCE = 128
D_FF = ((8 * D_MODEL + 3 * 256 - 1) // (3 * 256)) * 256
QKV_WIDTH = (N_HEADS + 2 * N_KV_HEADS) * HEAD_DIM
RMS_EPS = 1e-6
LN_EPS = 1e-5
NEG_INF = -1e30


def rms_norm(x, g):
    xf = x.astype(jnp.float32)
    y = xf * lax.rsqrt(jnp.mean(xf * xf, axis=-1, keepdims=True) + RMS_EPS)
    return (y * g.astype(jnp.float32)).astype(x.dtype)

def layer_norm(x, g, b):
    xf = x.astype(jnp.float32)
    mu = jnp.mean(xf, axis=-1, keepdims=True)
    var = jnp.mean(jnp.square(xf - mu), axis=-1, keepdims=True)
    y = (xf - mu) * lax.rsqrt(var + LN_EPS)
    return (y * g.astype(jnp.float32) + b.astype(jnp.float32)).astype(x.dtype)

def t5_bucket(dist):
    max_exact = N_BUCKETS // 2
    d = jnp.maximum(dist, max_exact).astype(jnp.float32)
    large = max_exact + (jnp.log(d / max_exact) / math.log(MAX_DISTANCE / max_exact)
                         * (N_BUCKETS - max_exact)).astype(jnp.int32)
    return jnp.where(dist < max_exact, dist, jnp.minimum(large, N_BUCKETS - 1))

def rel_bias_lookup(rel_bias, dist):
    b = rel_bias.astype(jnp.float32)[t5_bucket(dist)]
    b = jnp.moveaxis(b, -1, -3)
    return b.reshape(b.shape[:-3] + (N_KV_HEADS, GROUP) + b.shape[-2:])

def sink_softmax(scores, sinks):
    sink = jnp.broadcast_to(sinks[None, :, :, None, None], scores.shape[:-1] + (1,))
    p = jax.nn.softmax(jnp.concatenate([scores, sink], axis=-1), axis=-1)
    return p[..., :-1]

def conformer_conv(h, w_in, b_in, w_dw, b_dw, ln_g, ln_b, w_out, b_out):
    u = h @ w_in + b_in
    a, g = jnp.split(u, 2, axis=-1)
    u = a * jax.nn.sigmoid(g)
    u = jnp.pad(u, ((0, 0), (CONV_WIDTH - 1, 0), (0, 0)))
    u = lax.conv_general_dilated(
        u, w_dw[:, None, :].astype(u.dtype), window_strides=(1,), padding='VALID',
        dimension_numbers=('NWC', 'WIO', 'NWC'), feature_group_count=D_MODEL) + b_dw
    u = layer_norm(u, ln_g, ln_b)
    u = jax.nn.silu(u)
    return u @ w_out + b_out

def sliding_window_sink_attention(h, w_qkv, b_qkv, sinks, w_o, b_o, rel_bias):
    B, L, _ = h.shape
    S = L - N_META
    n_blk = S // BLOCK
    qkv = h @ w_qkv + b_qkv
    q, k, v = jnp.split(qkv, [N_HEADS * HEAD_DIM, (N_HEADS + N_KV_HEADS) * HEAD_DIM], axis=-1)
    q = q.reshape(B, L, N_KV_HEADS, GROUP, HEAD_DIM) * (HEAD_DIM ** -0.5)
    k = k.reshape(B, L, N_KV_HEADS, HEAD_DIM)
    v = v.reshape(B, L, N_KV_HEADS, HEAD_DIM)
    sink_logits = sinks.astype(jnp.float32).reshape(N_KV_HEADS, GROUP)
    q_m, q_r = q[:, :N_META], q[:, N_META:]
    k_m, k_r = k[:, :N_META], k[:, N_META:]
    v_m, v_r = v[:, :N_META], v[:, N_META:]

    d_mm = jnp.arange(N_META)[:, None] - jnp.arange(N_META)[None, :]
    s_mm = (jnp.einsum('bqhgd,bkhd->bhgqk', q_m, k_m).astype(jnp.float32)
            + rel_bias_lookup(rel_bias, jnp.maximum(d_mm, 0)))
    s_mm = jnp.where(d_mm >= 0, s_mm, NEG_INF)
    p_mm = sink_softmax(s_mm, sink_logits).astype(v.dtype)
    o_m = jnp.einsum('bhgqk,bkhd->bqhgd', p_mm, v_m)

    pad = ((0, 0), (BLOCK, 0), (0, 0), (0, 0))
    k_p = jnp.pad(k_r, pad).reshape(B, n_blk + 1, BLOCK, N_KV_HEADS, HEAD_DIM)
    v_p = jnp.pad(v_r, pad).reshape(B, n_blk + 1, BLOCK, N_KV_HEADS, HEAD_DIM)
    k_band = jnp.concatenate([k_p[:, :-1], k_p[:, 1:]], axis=2)
    v_band = jnp.concatenate([v_p[:, :-1], v_p[:, 1:]], axis=2)
    q_blk = q_r.reshape(B, n_blk, BLOCK, N_KV_HEADS, GROUP, HEAD_DIM)

    qpos = jnp.arange(BLOCK)[:, None]
    kpos = jnp.arange(2 * BLOCK)[None, :]
    mpos = jnp.arange(N_META)[None, :]
    d_band = BLOCK + qpos - kpos
    in_window = (d_band >= 0) & (d_band < WINDOW)
    bias_band = rel_bias_lookup(rel_bias, jnp.maximum(d_band, 0))

    def block_fn(args):
        n, q_n, k_n, v_n = args
        valid = in_window & (n * BLOCK + kpos >= BLOCK)
        d_meta = N_META + n * BLOCK + qpos - mpos
        s_meta = (jnp.einsum('bqhgd,bmhd->bhgqm', q_n, k_m).astype(jnp.float32)
                  + rel_bias_lookup(rel_bias, d_meta))
        s_band = jnp.einsum('bqhgd,bjhd->bhgqj', q_n, k_n).astype(jnp.float32) + bias_band
        s_band = jnp.where(valid, s_band, NEG_INF)
        p = sink_softmax(jnp.concatenate([s_meta, s_band], axis=-1), sink_logits).astype(v_n.dtype)
        return (jnp.einsum('bhgqm,bmhd->bqhgd', p[..., :N_META], v_m)
                + jnp.einsum('bhgqj,bjhd->bqhgd', p[..., N_META:], v_n))

    xs = (jnp.arange(n_blk, dtype=jnp.int32), jnp.moveaxis(q_blk, 1, 0),
          jnp.moveaxis(k_band, 1, 0), jnp.moveaxis(v_band, 1, 0))
    o_r = lax.map(block_fn, xs)
    o_r = jnp.moveaxis(o_r, 0, 1).reshape(B, S, N_HEADS * HEAD_DIM)
    o = jnp.concatenate([o_m.reshape(B, N_META, N_HEADS * HEAD_DIM), o_r], axis=1)
    return o @ w_o + b_o

def swiglu(h, w_gate, w_up, w_down):
    return (jax.nn.silu(h @ w_gate) * (h @ w_up)) @ w_down

def first_inputs(seed: int = 0) -> dict:
    key = jax.random.key(seed)
    ks = list(jax.random.split(key, 24))
    n_conv = len(range(0, DEPTH, N_MIXERS))
    n_attn = len(range(1, DEPTH, N_MIXERS))
    D, F, H = D_MODEL, D_FF, N_HEADS * HEAD_DIM

    def nrm(k, shape, scale):
        return jax.random.normal(k, shape, jnp.float32) * scale

    def gain(k, shape):
        return 1.0 + nrm(k, shape, 0.02)

    return {
        'x': nrm(ks[0], (BATCH, SEQ, D), 1.0),
        'meta_tokens': nrm(ks[1], (N_META, D), 1.0),
        'rel_bias': nrm(ks[2], (N_BUCKETS, N_HEADS), 0.5),
        'conv_w_in': nrm(ks[3], (n_conv, D, 2 * D), D ** -0.5),
        'conv_b_in': nrm(ks[4], (n_conv, 2 * D), 0.02),
        'conv_w_dw': nrm(ks[5], (n_conv, CONV_WIDTH, D), CONV_WIDTH ** -0.5),
        'conv_b_dw': nrm(ks[6], (n_conv, D), 0.02),
        'conv_ln_g': gain(ks[7], (n_conv, D)),
        'conv_ln_b': nrm(ks[8], (n_conv, D), 0.02),
        'conv_w_out': nrm(ks[9], (n_conv, D, D), D ** -0.5),
        'conv_b_out': nrm(ks[10], (n_conv, D), 0.02),
        'attn_w_qkv': nrm(ks[11], (n_attn, D, QKV_WIDTH), D ** -0.5),
        'attn_b_qkv': nrm(ks[12], (n_attn, QKV_WIDTH), 0.02),
        'attn_sinks': nrm(ks[13], (n_attn, N_HEADS), 0.5),
        'attn_w_o': nrm(ks[14], (n_attn, H, D), H ** -0.5),
        'attn_b_o': nrm(ks[15], (n_attn, D), 0.02),
        'norm_mix_pre': gain(ks[16], (DEPTH, D)),
        'norm_mix_post': gain(ks[17], (DEPTH, D)),
        'norm_ffn_pre': gain(ks[18], (DEPTH, D)),
        'norm_ffn_post': gain(ks[19], (DEPTH, D)),
        'ffn_w_gate': nrm(ks[20], (DEPTH, D, F), D ** -0.5),
        'ffn_w_up': nrm(ks[21], (DEPTH, D, F), D ** -0.5),
        'ffn_w_down': nrm(ks[22], (DEPTH, F, D), F ** -0.5),
    }

def first_block(x, meta_tokens, rel_bias, conv_w_in, conv_b_in, conv_w_dw, conv_b_dw,
              conv_ln_g, conv_ln_b, conv_w_out, conv_b_out, attn_w_qkv, attn_b_qkv,
              attn_sinks, attn_w_o, attn_b_o, norm_mix_pre, norm_mix_post,
              norm_ffn_pre, norm_ffn_post, ffn_w_gate, ffn_w_up, ffn_w_down):
    B = x.shape[0]
    meta = jnp.broadcast_to(meta_tokens.astype(x.dtype)[None], (B, N_META, D_MODEL))
    h = jnp.concatenate([meta, x], axis=1)
    for i in range(DEPTH):
        j = i // N_MIXERS
        u = rms_norm(h, norm_mix_pre[i])
        if i % N_MIXERS == 0:
            u = conformer_conv(u, conv_w_in[j], conv_b_in[j], conv_w_dw[j], conv_b_dw[j],
                               conv_ln_g[j], conv_ln_b[j], conv_w_out[j], conv_b_out[j])
        else:
            u = sliding_window_sink_attention(u, attn_w_qkv[j], attn_b_qkv[j], attn_sinks[j],
                                              attn_w_o[j], attn_b_o[j], rel_bias)
        h = h + rms_norm(u, norm_mix_post[i])
        u = swiglu(rms_norm(h, norm_ffn_pre[i]), ffn_w_gate[i], ffn_w_up[i], ffn_w_down[i])
        h = h + rms_norm(u, norm_ffn_post[i])
    return h[:, N_META:]


CHUNK = 64
CONV_WIDTH_2 = 1024
CONV_K = 3
SGU_WIDTH = 1024
SGU_HEADS = 8
SGU_HEAD_DIM = SGU_WIDTH // SGU_HEADS
SGU_BLOCK = 128
N_BRANCH = 2
IN_COLS = 3 * CONV_WIDTH_2 + 2 * SGU_WIDTH + N_BRANCH * D_MODEL
N_GROUPS = 4
EXPERTS_PER_GROUP = 4
N_EXPERTS = N_GROUPS * EXPERTS_PER_GROUP
TOP_K_INNER = 2
D_EXPERT = D_MODEL // 4
EPS = 1e-6


def rms_norm_2(x, g):
    xf = x.astype(jnp.float32)
    y = xf * lax.rsqrt(jnp.mean(xf * xf, axis=-1, keepdims=True) + EPS)
    return (y * g.astype(jnp.float32)).astype(x.dtype)

def layer_norm_2(x, g, b):
    xf = x.astype(jnp.float32)
    mu = jnp.mean(xf, axis=-1, keepdims=True)
    xc = xf - mu
    y = xc * lax.rsqrt(jnp.mean(xc * xc, axis=-1, keepdims=True) + EPS)
    return (y * g.astype(jnp.float32) + b.astype(jnp.float32)).astype(x.dtype)

def causal_depthwise_conv(z, w):
    c = z.shape[-1]
    return lax.conv_general_dilated(
        z, w[:, None, :].astype(z.dtype), window_strides=(1,),
        padding=[(CONV_K - 1, 0)], dimension_numbers=('NWC', 'WIO', 'NWC'),
        feature_group_count=c)

def short_conv_mixer(b_gate, c_gate, h_in, conv_w):
    return b_gate * causal_depthwise_conv(c_gate * h_in, conv_w)

def spatial_gating_mixer(z, ln_g, ln_b, w_s, b_s):
    bsz, s, _ = z.shape
    z = jax.nn.gelu(z)
    u, v = jnp.split(z, 2, axis=-1)
    v = layer_norm_2(v, ln_g, ln_b)
    chunk_id = jnp.arange(SGU_BLOCK) // CHUNK
    mask = chunk_id[None, :] <= chunk_id[:, None]
    w = jnp.where(mask[None], w_s, jnp.zeros_like(w_s)).astype(v.dtype)
    vb = v.reshape(bsz, s // SGU_BLOCK, SGU_BLOCK, SGU_HEADS, SGU_HEAD_DIM)
    vm = jnp.einsum('hij,bnjhc->bnihc', w, vb) + b_s.T.astype(v.dtype)[:, :, None]
    return u * vm.reshape(bsz, s, SGU_WIDTH)

def hierarchical_moe(x, w_rg, b_rg, w_re, b_re, w_gate, w_up, w_down):
    bsz, s, d = x.shape
    t = x.reshape(-1, d)
    tf = t.astype(jnp.float32)
    p_group = jax.nn.softmax(tf @ w_rg.astype(jnp.float32) + b_rg.astype(jnp.float32), axis=-1)
    pg, g_idx = lax.top_k(p_group, 1)
    oh_g = jax.nn.one_hot(g_idx[:, 0], N_GROUPS, dtype=jnp.float32)
    exp_logits = (tf @ w_re.astype(jnp.float32) + b_re.astype(jnp.float32)).reshape(-1, N_GROUPS, EXPERTS_PER_GROUP)
    sel_logits = jnp.einsum('tg,tge->te', oh_g, exp_logits)
    pe, e_idx = lax.top_k(jax.nn.softmax(sel_logits, axis=-1), TOP_K_INNER)
    pe = pe / jnp.sum(pe, axis=-1, keepdims=True)
    w_inner = jnp.einsum('tk,tke->te', pe, jax.nn.one_hot(e_idx, EXPERTS_PER_GROUP, dtype=jnp.float32))
    gate = ((pg * oh_g)[:, :, None] * w_inner[:, None, :]).reshape(-1, N_EXPERTS).astype(x.dtype)
    hid = jax.nn.silu(jnp.einsum('td,edf->tef', t, w_gate)) * jnp.einsum('td,edf->tef', t, w_up)
    y = jnp.einsum('tef,efd->td', hid * gate[:, :, None], w_down)
    return y.reshape(bsz, s, d)

def second_inputs(seed: int = 0) -> dict:
    key = jax.random.key(seed)
    ks = jax.random.split(key, 20)
    f32 = jnp.float32
    nrm = lambda k, shape, scale: jax.random.normal(k, shape, f32) * scale
    L = DEPTH
    return {
        'x': jax.random.normal(ks[0], (BATCH, SEQ, D_MODEL), f32),
        'norm_mix_g': 1.0 + nrm(ks[1], (L, D_MODEL), 0.02),
        'w_in': nrm(ks[2], (L, D_MODEL, IN_COLS), D_MODEL ** -0.5),
        'conv_w': nrm(ks[3], (L, CONV_K, CONV_WIDTH_2), CONV_K ** -0.5),
        'sgu_ln_g': 1.0 + nrm(ks[4], (L, SGU_WIDTH), 0.02),
        'sgu_ln_b': nrm(ks[5], (L, SGU_WIDTH), 0.02),
        'sgu_w_s': nrm(ks[6], (L, SGU_HEADS, SGU_BLOCK, SGU_BLOCK), SGU_BLOCK ** -0.5),
        'sgu_b_s': 1.0 + nrm(ks[7], (L, SGU_HEADS, SGU_BLOCK), 0.02),
        'w_up_conv': nrm(ks[8], (L, CONV_WIDTH_2, D_MODEL), CONV_WIDTH_2 ** -0.5),
        'w_up_sgu': nrm(ks[9], (L, SGU_WIDTH, D_MODEL), SGU_WIDTH ** -0.5),
        'w_out': nrm(ks[10], (L, D_MODEL, D_MODEL), D_MODEL ** -0.5),
        'norm_ffn_g': 1.0 + nrm(ks[11], (L, D_MODEL), 0.02),
        'w_router_group': nrm(ks[12], (L, D_MODEL, N_GROUPS), D_MODEL ** -0.5),
        'b_router_group': nrm(ks[13], (L, N_GROUPS), 0.01),
        'w_router_expert': nrm(ks[14], (L, D_MODEL, N_EXPERTS), D_MODEL ** -0.5),
        'b_router_expert': nrm(ks[15], (L, N_EXPERTS), 0.01),
        'w_exp_gate': nrm(ks[16], (L, N_EXPERTS, D_MODEL, D_EXPERT), D_MODEL ** -0.5),
        'w_exp_up': nrm(ks[17], (L, N_EXPERTS, D_MODEL, D_EXPERT), D_MODEL ** -0.5),
        'w_exp_down': nrm(ks[18], (L, N_EXPERTS, D_EXPERT, D_MODEL), D_EXPERT ** -0.5),
        'norm_final_g': 1.0 + nrm(ks[19], (D_MODEL,), 0.02),
    }

def second_block(x, norm_mix_g, w_in, conv_w, sgu_ln_g, sgu_ln_b, sgu_w_s, sgu_b_s,
              w_up_conv, w_up_sgu, w_out, norm_ffn_g, w_router_group, b_router_group,
              w_router_expert, b_router_expert, w_exp_gate, w_exp_up, w_exp_down,
              norm_final_g):
    h = x
    splits = [CONV_WIDTH_2, 2 * CONV_WIDTH_2, 3 * CONV_WIDTH_2, 3 * CONV_WIDTH_2 + 2 * SGU_WIDTH]
    for l in range(DEPTH):
        xn = rms_norm_2(h, norm_mix_g[l])
        proj = xn @ w_in[l]
        b_c, c_c, h_c, z_s, gate_logits = jnp.split(proj, splits, axis=-1)
        y_conv = short_conv_mixer(b_c, c_c, h_c, conv_w[l]) @ w_up_conv[l]
        y_sgu = spatial_gating_mixer(z_s, sgu_ln_g[l], sgu_ln_b[l], sgu_w_s[l], sgu_b_s[l]) @ w_up_sgu[l]
        g_conv, g_sgu = jnp.split(jax.nn.sigmoid(gate_logits), 2, axis=-1)
        h = h + (g_conv * y_conv + g_sgu * y_sgu) @ w_out[l]
        h = h + hierarchical_moe(rms_norm_2(h, norm_ffn_g[l]), w_router_group[l], b_router_group[l],
                                 w_router_expert[l], b_router_expert[l],
                                 w_exp_gate[l], w_exp_up[l], w_exp_down[l])
    return rms_norm_2(h, norm_final_g)


def setup_inputs(seed=0):
    out = dict(first_inputs(seed))
    for name, value in second_inputs(seed + 1).items():
        if name != "x":
            out[name + "_2"] = value
    return out


def reference(
    x, meta_tokens, rel_bias, conv_w_in, conv_b_in, conv_w_dw, conv_b_dw, conv_ln_g, conv_ln_b,
    conv_w_out, conv_b_out, attn_w_qkv, attn_b_qkv, attn_sinks, attn_w_o, attn_b_o,
    norm_mix_pre, norm_mix_post, norm_ffn_pre, norm_ffn_post, ffn_w_gate, ffn_w_up, ffn_w_down,
    norm_mix_g_2, w_in_2, conv_w_2, sgu_ln_g_2, sgu_ln_b_2, sgu_w_s_2, sgu_b_s_2, w_up_conv_2,
    w_up_sgu_2, w_out_2, norm_ffn_g_2, w_router_group_2, b_router_group_2, w_router_expert_2,
    b_router_expert_2, w_exp_gate_2, w_exp_up_2, w_exp_down_2, norm_final_g_2,
):
    x = first_block(
        x, meta_tokens, rel_bias, conv_w_in, conv_b_in, conv_w_dw, conv_b_dw, conv_ln_g,
        conv_ln_b, conv_w_out, conv_b_out, attn_w_qkv, attn_b_qkv, attn_sinks, attn_w_o,
        attn_b_o, norm_mix_pre, norm_mix_post, norm_ffn_pre, norm_ffn_post, ffn_w_gate,
        ffn_w_up, ffn_w_down,
    )
    return second_block(
        x, norm_mix_g_2, w_in_2, conv_w_2, sgu_ln_g_2, sgu_ln_b_2, sgu_w_s_2, sgu_b_s_2,
        w_up_conv_2, w_up_sgu_2, w_out_2, norm_ffn_g_2, w_router_group_2, b_router_group_2,
        w_router_expert_2, b_router_expert_2, w_exp_gate_2, w_exp_up_2, w_exp_down_2,
        norm_final_g_2,
    )


_drawn_inputs = setup_inputs


def setup_inputs(seed=0):
    import zlib

    import numpy as np

    out = dict(_drawn_inputs(seed))
    spreads = {}
    factors = {'norm_ffn_post': 3.191,
     'norm_mix_g_2': 3.529,
     'sgu_ln_g_2': 8.0,
     'sgu_ln_b_2': 29.941,
     'sgu_b_s_2': 6.987,
     'norm_ffn_g_2': 4.716,
     'b_router_group_2': 4.571,
     'b_router_expert_2': 64.0,
     'norm_final_g_2': 7.892}
    for name, (base, spread) in spreads.items():
        noise = np.random.default_rng([zlib.crc32(name.encode()), seed]).standard_normal(out[name].shape)
        drawn = base * np.exp(spread * noise) if base else spread * noise
        out[name] = jnp.asarray(drawn.astype(out[name].dtype))
    for name, factor in factors.items():
        out[name] = (out[name] * factor).astype(out[name].dtype)
    return out
```

```python
from contextlib import ExitStack, contextmanager

import concourse.bass as bass
from concourse import mybir

ALU = mybir.AluOpType
ACT = mybir.ActivationFunctionType
AX_X = mybir.AxisListType.X
F32 = mybir.dt.float32
F32R = mybir.dt.float32r
BF16 = mybir.dt.bfloat16
I32 = mybir.dt.int32

P = 128
PANEL = 2048
RING = 4
BANK = 512
ds = bass.ds


class Tally:

    def __init__(self, sem):
        self.sem, self.base, self.k = sem, 0, 0

    def mark(self, instruction):
        instruction.then_inc(self.sem, 1)
        self.k += 1

    def wait(self, eng, back=0):
        eng.wait_ge(self.sem, self.base + (self.k - back))


@contextmanager
def rounds(eng, count, *counted):
    before = [t.k for t, _ in counted]
    assert all(isinstance(t.base, int) and t.base == 0 for t, _ in counted)
    with eng.Fori(0, count) as i:
        for t, per in counted:
            t.base = i * per
        yield i
    for (t, per), k in zip(counted, before):
        assert t.k == k + per, (t.k - k, per)
        t.base, t.k = 0, k + per * count


def build_program(
    nc, x, meta_tokens, conv_w_in, conv_b_in, conv_w_dw, conv_b_dw, conv_ln_g, conv_ln_b,
    conv_w_out, conv_b_out, norm_mix_pre, norm_mix_post, norm_ffn_pre, norm_ffn_post,
    ffn_w_gate, ffn_w_up, ffn_w_down, norm_mix_g_2, w_in_2, conv_w_2, sgu_ln_g_2, sgu_ln_b_2,
    sgu_w_s_2, sgu_b_s_2, w_up_conv_2, w_up_sgu_2, w_out_2, norm_ffn_g_2, w_router_group_2,
    b_router_group_2, w_router_expert_2, b_router_expert_2, w_exp_gate_2, w_exp_up_2,
    w_exp_down_2, norm_final_g_2, out,
):
    D = x.shape[2]
    T = x.shape[1]
    META = meta_tokens.shape[0]
    TM = META + T
    KT = D // P
    TOK = T // P
    NC = D // BANK
    FF = ffn_w_down.shape[1]
    FT = FF // P
    TAPS = conv_w_dw.shape[1]
    PAD = TAPS - 1 - META
    EXT = PAD + TM
    CW = conv_w_2.shape[2]
    CT = CW // P
    SW = sgu_ln_g_2.shape[1]
    HEADS = sgu_w_s_2.shape[1]
    SBLK = sgu_w_s_2.shape[2]
    HALF = SBLK // 2
    GROUPS = w_router_group_2.shape[2]
    EXPERTS = w_exp_gate_2.shape[1]
    PER = EXPERTS // GROUPS
    DE = w_exp_gate_2.shape[3]
    ET = DE // P
    RMS_EPS, LN_EPS, EPS = 1e-6, 1e-5, 1e-6
    GELU_A = 1.5957691216057308
    GELU_B = GELU_A * 0.044715
    assert T == 2 * P and D == PANEL and SW == HEADS * P and SBLK == P and PAD >= 0 and CW == SW

    A = 0
    B = A + 2 * KT
    C = B + KT
    DN = C + 2 * FT
    ZV = DN + FT
    CH = ZV + 8
    BG = CH + 2 * CT
    U = BG + CT
    GT = U + CT
    UP = GT + 2 * KT
    G = UP + 2 * CT
    MOE = G + KT
    JOB = 3 * PER * ET
    S_B, S_D, S_G = 0, KT, KT + FT
    F_C, F_E = 0, 2 * FT
    F_UP = F_E + (UP - CH)
    F_END = F_UP + 4 * CT

    ctx = ExitStack()
    with ctx:
        arena_at = -(-nc.sbuf_base // 32) * 32

        def sb(name, shape, dt=F32):
            return ctx.enter_context(nc.sbuf_tensor(name, shape, dt))

        def sem(name):
            return ctx.enter_context(nc.semaphore(name))

        BIG = FT * T
        big = sb("big", [P, BIG])
        MR = 2 * KT * P + 2 * D + 2 * P + 2 * P + 2 * ET * P
        moe_r = nc.alloc_sbuf_tensor_at("moe_r", [P, MR], F32R, offset=arena_at)
        moe_f = nc.alloc_sbuf_tensor_at("moe_f", [P, BIG - MR], F32, offset=arena_at + 4 * MR)
        raw = sb("raw", [P, RING, PANEL])
        whi = sb("whi", [P, 2, PANEL], F32R)
        wlo = sb("wlo", [P, 2, PANEL], F32R)
        xT = sb("xT", [P, KT * 2 * TM], F32R)
        h = sb("h", [P, TOK, D])
        tmp = sb("tmp", [P, TOK, D])
        gB = sb("gB", [P, D])
        act = sb("act", [P, 2, 2, T], F32R)
        vT = sb("vT", [P, 6, P])
        ident = sb("ident", [P, P])
        ones = sb("ones", [P, P])
        wsT = sb("wsT", [P, HEADS, P])
        bsB = sb("bsB", [P, HEADS, P])
        wr = sb("wr", [P, KT, GROUPS + EXPERTS])
        wk = sb("wk", [P, 7 * T])
        st = sb("st", [P, 96])
        sti = sb("sti", [P, 2], I32)
        brow = sb("brow", [1, GROUPS + EXPERTS])
        zrow = sb("zrow", [1, BANK], BF16)
        ps = ctx.enter_context(nc.psum_tensor("ps", [P, 8, BANK], F32))

        xTA = xT[:, :].rearrange("p (k c) -> p k c", k=KT)
        xT5 = xT[:, 0:KT * BANK].rearrange("p (k c) -> p k c", k=KT)
        tH = xT[:, 0:TOK * D].rearrange("p (t d) -> p t d", t=TOK)
        tL = xT[:, TOK * D:2 * TOK * D].rearrange("p (t d) -> p t d", t=TOK)
        uext = big[:, 0:KT * EXT].rearrange("p (k c) -> p k c", k=KT)
        conv_at = KT * EXT + 32
        cv = big[:, conv_at:conv_at + KT * T].rearrange("p (k c) -> p k c", k=KT)
        stage_at = conv_at + KT * T
        vst = big[:, stage_at:stage_at + 6 * P].rearrange("p (r c) -> p r c", r=6)
        wst = big[:, stage_at + 6 * P:stage_at + 6 * P + HEADS * P].rearrange("p (r c) -> p r c", r=HEADS)
        tiles = big[:, :].rearrange("p (k c) -> p k c", c=T)
        UT = 2 * KT
        pext_at = (UT + CT) * T
        pext = big[:, pext_at:pext_at + 2 * (T + 2)].rearrange("p (s c) -> p s c", s=2)
        vbuf = tmp[:, 0, :].rearrange("p (t c) -> p t c", t=TOK)
        vmb = tmp[:, 0, :]
        vscr = tmp[:, 1, :]
        yc = tmp[:, 1, :].rearrange("p (k c) -> p k c", k=CT)
        t1 = wk[:, 0:2 * T].rearrange("p (s c) -> p s c", s=2)
        xs = wk[:, 2 * T:5 * T].rearrange("p (s c) -> p s c", s=3)
        sg = wk[:, 5 * T:7 * T].rearrange("p (s c) -> p s c", s=2)
        sgA = wk[:, 0:2 * TM].rearrange("p (s c) -> p s c", s=2)
        meanb, rstdb = wk[:, 0:T], wk[:, T:2 * T]
        xg = moe_r[:, 0:2 * KT * P].rearrange("p (o k c) -> p o k c", o=2, k=KT)
        yh = moe_r[:, 2 * KT * P:2 * KT * P + 2 * D].rearrange("p (o c) -> p o c", o=2)
        S_at = 2 * KT * P + 2 * D
        Sel = moe_r[:, S_at:S_at + 2 * P].rearrange("p (t c) -> p t c", t=TOK)
        SelT = moe_r[:, S_at + 2 * P:S_at + 4 * P].rearrange("p (t c) -> p t c", t=TOK)
        hT = moe_r[:, S_at + 4 * P:S_at + 4 * P + 2 * ET * P].rearrange("p (o k c) -> p o k c", o=2, k=ET)
        iota = moe_f[:, 0:P]
        gsl = moe_f[:, P:P + DE]
        hid = moe_f[:, P + DE:P + 2 * DE]
        V_PRE, V_BIN, V_BDW, V_LG, V_LB, V_FPRE, V_MIX2 = 0, 16, 48, 64, 80, 96, 112
        V_DW = P
        V_CW2 = 5 * P
        vcol = vT[:, :, :].rearrange("p r c -> p (r c)")

        SSQ, SS, RT, RS, MV, BN, SLOTW = 0, 8, 12, 16, 20, 24, 48
        EPS_AT, LN_EPS_AT = 88, 89
        OHG = TOK * (GROUPS + EXPERTS) + 2 + 2 * 4 * TOK
        GATE = OHG + 4 * 4 * TOK

        raw_in = [sem(f"raw_in{i}") for i in range(RING)]
        hi_ready = sem("hi_ready")
        lo_pool = sem("lo_pool")
        lo_ready = sem("lo_ready")
        mm_done = sem("mm_done")
        x_in = sem("x_in")
        meta_in = sem("meta_in")
        vec_in = sem("vec_in")
        ws_in = sem("ws_in")
        bs_in = sem("bs_in")
        wr_in = sem("wr_in")
        gain_in = sem("gain_in")
        ident_ready = sem("ident_ready")
        ones_ready = sem("ones_ready")
        vec_turned = sem("vec_turned")
        vec_ready = sem("vec_ready")
        ws_turned = sem("ws_turned")
        ws_ready = sem("ws_ready")
        ssq_ready = sem("ssq_ready")
        root_ready = sem("root_ready")
        var_ready = sem("var_ready")
        xn_ready = sem("xn_ready")
        turned = sem("turned")
        xhi_ready = sem("xhi_ready")
        xlo_ready = sem("xlo_ready")
        pad_ready = sem("pad_ready")
        sig_a = sem("sig_a")
        glu_done = sem("glu_done")
        conv_done = sem("conv_done")
        sums_done = sem("sums_done")
        cent = sem("cent")
        sq_done = sem("sq_done")
        z_ready = sem("z_ready")
        zs_ready = sem("zs_ready")
        u_ready = sem("u_ready")
        open_done = sem("open_done")
        act_hi = sem("act_hi")
        act_lo = sem("act_lo")
        post_done = sem("post_done")
        feat_half = sem("feat_half")
        feat_free = sem("feat_free")
        sig_c = sem("sig_c")
        hid_ready = sem("hid_ready")
        vsq = sem("vsq")
        varg = sem("varg")
        vsig = sem("vsig")
        v_free = sem("v_free")
        v_norm = sem("v_norm")
        v_ready = sem("v_ready")
        spat_done = sem("spat_done")
        vm_ready = sem("vm_ready")
        usq = sem("usq")
        uarg = sem("uarg")
        usig = sem("usig")
        ut_ready = sem("ut_ready")
        gate_ready = sem("gate_ready")
        ys_ready = sem("ys_ready")
        fused_done = sem("fused_done")
        bias_in = sem("bias_in")
        pair_hi = sem("pair_hi")
        pair_lo = sem("pair_lo")
        thi_ready = sem("thi_ready")
        tlo_ready = sem("tlo_ready")
        tt_turned = sem("tt_turned")
        tt_ready = sem("tt_ready")
        logits_done = sem("logits_done")
        r_shift = sem("r_shift")
        r_exp = sem("r_exp")
        r_mask = sem("r_mask")
        rank_done = sem("rank_done")
        jobs_ready = sem("jobs_ready")
        tri_ready = sem("tri_ready")
        sel_ready = sem("sel_ready")
        slot_done = sem("slot_done")
        selT_ready = sem("selT_ready")
        gath_hi = sem("gath_hi")
        gath_lo = sem("gath_lo")
        xg_hi = sem("xg_hi")
        xg_lo = sem("xg_lo")
        sig_g = sem("sig_g")
        gsl_ready = sem("gsl_ready")
        hid_e = sem("hid_e")
        hid_turned = sem("hid_turned")
        hT_hi = sem("hT_hi")
        hT_lo = sem("hT_lo")
        y_hi = sem("y_hi")
        y_lo = sem("y_lo")
        scat_done = sem("scat_done")
        add_done = sem("add_done")
        fin_ready = sem("fin_ready")
        out_done = sem("out_done")
        act_own = sem("act_own")
        dve_own = sem("dve_own")
        pool_own = sem("pool_own")

        w_exp_g = w_exp_gate_2.rearrange("l e d f -> (l e d) f")
        w_exp_u = w_exp_up_2.rearrange("l e d f -> (l e d) f")
        w_exp_d = w_exp_down_2.rearrange("l e f d -> (l e f) d")

        block = ctx.enter_context(nc.Block())

        @block.sync
        def _(sp):
            def panel(n, s, src, rows, first=False):
                slot = s % RING
                if not first:
                    if isinstance(n, int) and n + s - RING < B:
                        sp.wait_ge(lo_pool, n + s - RING + 1)
                    else:
                        sp.wait_ge(lo_ready, n + (s - RING - B + 1))
                dst = raw[:, slot, :].rearrange("p (k c) -> p k c", c=rows)
                sp.dma_start(dst, src).then_inc(raw_in[slot], 16)

            def columns(w, c, width=P):
                return w[:, ds(c, width)].rearrange("(k p) n -> p k n", p=P)

            def rows_of(w, r):
                return w[ds(r, P), :].rearrange("(a p) n -> p a n", p=P)

            w_in = conv_w_in[0]
            for s in range(4):
                m, g = divmod(s, 2)
                panel(0, s, columns(w_in, g * D + m * P), P, first=True)
            with sp.Fori(1, B // 4) as r:
                n = r * 4
                for s in range(4):
                    m, g = divmod(s, 2)
                    slot = s
                    sp.wait_ge(lo_pool, n + (s - RING + 1))
                    dst = raw[:, slot, :].rearrange("p (k c) -> p k c", c=P)
                    sp.dma_start(dst, columns(w_in, n * (P // 2) + (g * D + m * P))).then_inc(raw_in[slot], 16)
            for s in range(4):
                panel(B, s, rows_of(conv_w_out[0], s * P), D)
            with sp.Fori(1, (KT) // 4) as r:
                j = r * 4
                for s in range(4):
                    panel(j + B, s, rows_of(conv_w_out[0], (j + s) * P), D)
            with sp.Fori(0, (2 * FT) // 4) as r:
                j = r * 4
                for s in range(4):
                    m, g = divmod(s, 2)
                    panel(j + C, s, columns((ffn_w_gate, ffn_w_up)[g][0], j * (P // 2) + m * P), P)
            with sp.Fori(0, (FT) // 4) as r:
                j = r * 4
                for s in range(4):
                    panel(j + DN, s, rows_of(ffn_w_down[0], (j + s) * P), D)
            with sp.Fori(0, (8) // 4) as r:
                j = r * 4
                for s in range(4):
                    src = w_in_2[0, ds((j + s) * (2 * P), 2 * P), 3 * CW + SW:3 * CW + 2 * SW]
                    panel(j + ZV, s, src.rearrange("(k p) n -> p k n", p=P), SW)
            with sp.Fori(0, (2 * CT) // 4) as r:
                j = r * 4
                for s in range(4):
                    m, g = divmod(s, 2)
                    panel(j + CH, s, columns(w_in_2[0], j * (P // 2) + (m * P + (1 + g) * CW)), P)
            for first, col, count in ((BG, 0, CT), (U, 3 * CW, CT), (GT, 3 * CW + 2 * SW, 2 * KT)):
                with sp.Fori(0, (count) // 4) as r:
                    j = r * 4
                    for s in range(4):
                        panel(j + first, s, columns(w_in_2[0], (j + s) * P + col), P)
            with sp.Fori(0, (2 * CT) // 4) as r:
                j = r * 4
                for s in range(4):
                    m, g = divmod(s, 2)
                    w = (w_up_conv_2, w_up_sgu_2)[g][0]
                    panel(j + UP, s, columns(w, j * P + m * 2 * P, 2 * P), 2 * P)
            with sp.Fori(0, (KT) // 4) as r:
                j = r * 4
                for s in range(4):
                    panel(j + G, s, rows_of(w_out_2[0], (j + s) * P), D)

            def expert_in(w, n, s0, e):
                for q in range(4):
                    src = w[ds(e * D + q * (ET * P), ET * P), :].rearrange("(k p) f -> p k f", p=P)
                    panel(n, s0 + q, src, DE)

            def expert_down(n, s0, e):
                for r in range(ET):
                    panel(n, s0 + r, w_exp_d[ds(e * DE + r * P, P), :].rearrange("(a p) n -> p a n", p=P), D)

            def job(n, e0):
                expert_in(w_exp_g, n, 0, e0)
                expert_in(w_exp_u, n, 4, e0)
                with sp.Fori(0, PER - 1) as e:
                    expert_in(w_exp_g, n + e * 12, 8, e0 + e + 1)
                    expert_in(w_exp_u, n + e * 12, 12, e0 + e + 1)
                    expert_down(n + e * 12, 16, e0 + e)
                expert_down(n, JOB - 4, e0 + (PER - 1))

            with sp.Fori(0, GROUPS) as g:
                job(g * JOB + MOE, g * PER)
            sp.wait_ge(jobs_ready, 1)
            extra = nc.sync.value_load(sti[0:1, 0:1], min_val=GROUPS, max_val=GROUPS + 1)
            over = nc.sync.value_load(sti[0:1, 1:2], min_val=0, max_val=GROUPS - 1)
            with sp.If(extra > GROUPS):
                job(MOE + GROUPS * JOB, over * PER)
            sp.end_ifs()
            sp.wait_ge(fin_ready, 2)
            sp.dma_start(out[0].rearrange("(t p) d -> p t d", p=P), tmp[:, :, :]).then_inc(out_done, 16)
            sp.wait_ge(out_done, 16)

        @block.gpsimd
        def _(pool):
            own = Tally(pool_own)
            own.mark(pool.memset(ident[:, :], 0.0))
            pool.memset(ones[:, :], 1.0).then_inc(ones_ready, 1)
            pool.memset(zrow[:, :], 0.0).then_inc(ones_ready, 1)
            own.wait(pool)
            pool.affine_select(out=ident[:, :], in_=ident[:, :], compare_op=ALU.not_equal, fill=1.0, base=0,
                               pattern=[[-1, P]], channel_multiplier=1).then_inc(ident_ready, 1)
            pool.dma_start(bsB[:, :, :].rearrange("p h i -> p (h i)"),
                           sgu_b_s_2.rearrange("l h i -> l (h i)").to_broadcast([P, HEADS * SBLK])).then_inc(bs_in, 16)

            pool.dma_start(brow[:, 0:GROUPS], b_router_group_2).then_inc(bias_in, 16)
            pool.dma_start(brow[:, GROUPS:GROUPS + EXPERTS], b_router_expert_2).then_inc(bias_in, 16)

            pool.wait_ge(ssq_ready, 3)
            pool.memset(uext[:, :, 0:PAD], 0.0).then_inc(pad_ready, 1)
            with pool.Fori(0, KT // 2) as r:
                n = r * 4
                for s in range(4):
                    pool.wait_ge(hi_ready, n + (s + 1))
                    pool.tensor_tensor(wlo[:, s % 2, :], raw[:, s, :], whi[:, s % 2, :], ALU.subtract).then_inc(lo_pool, 1)

            pool.wait_ge(turned, 16)
            pool.dma_start(gB[0:1, :], conv_b_out).then_inc(gain_in, 16)
            pool.wait_ge(open_done, 1)
            pool.dma_start(gB[:, :], norm_mix_post.to_broadcast([P, D])).then_inc(gain_in, 16)
            pool.wait_ge(post_done, 8)
            pool.dma_start(gB[:, :], norm_ffn_post.to_broadcast([P, D])).then_inc(gain_in, 16)
            pool.wait_ge(post_done, 16)
            pool.dma_start(gB[:, 0:SW], sgu_ln_g_2.to_broadcast([P, SW])).then_inc(gain_in, 16)
            pool.dma_start(gB[:, SW:2 * SW], sgu_ln_b_2.to_broadcast([P, SW])).then_inc(gain_in, 16)
            pool.wait_ge(gain_in, 80)
            for t in range(TOK):
                pool.wait_ge(v_norm, t + 1)
                own.mark(pool.tensor_tensor(vbuf[:, t, :], vbuf[:, t, :], gB[:, 0:SW], ALU.mult))
                own.wait(pool)
                pool.tensor_tensor(vbuf[:, t, :], vbuf[:, t, :], gB[:, SW:2 * SW], ALU.add).then_inc(v_ready, 1)
            pool.wait_ge(v_ready, 2)
            pool.dma_start(gB[:, :], norm_ffn_g_2.to_broadcast([P, D])).then_inc(gain_in, 16)
            pool.wait_ge(vm_ready, 4)
            for m in range(CT):
                pool.wait_ge(ut_ready, m + 1 + 2)
                pool.tensor_tensor(tiles[:, UT + m, :], tiles[:, UT + m, :], vmb[:, m * T:(m + 1) * T],
                                   ALU.mult).then_inc(ys_ready, 1)
            pool.wait_ge(xn_ready, 7 + 2)
            pool.dma_start(gB[:, :], norm_final_g_2.rearrange("(a d) -> a d", a=1).to_broadcast([P, D])).then_inc(gain_in, 16)
            pool.wait_ge(spat_done, 1)
            own.mark(pool.memset(wsT[:, 0, :], 1.0))
            own.wait(pool)
            pool.affine_select(out=wsT[:, 0, :], in_=wsT[:, 0, :], compare_op=ALU.is_gt, fill=0.0, base=0,
                               pattern=[[1, P]], channel_multiplier=-1).then_inc(tri_ready, 1)
            pool.wait_ge(mm_done, MOE)
            pool.iota(iota.bitcast(I32), pattern=[[1, P]], base=0, channel_multiplier=0).then_inc(tri_ready, 1)

        @block.scalar
        def _(a):
            own = Tally(act_own)
            fn = nc.scalar.activation

            def hi(n, s, s_slot=None):
                if not (isinstance(n, int) and n + s < 2):
                    a.wait_ge(mm_done, n + (s - 1))
                a.wait_ge(raw_in[s % RING], n * 4 + (16 * (s // RING) + 16))
                fn(whi[:, s % 2, :], raw[:, s % RING, :], ACT.Copy).then_inc(hi_ready, 1)

            def root(src, dst, scale, eps):
                fn(dst, src, ACT.Sqrt, bias=eps, scale=scale).then_inc(root_ready, 1)

            for t in range(TOK):
                a.dma_start(h[:, t, :], x[0, t * P:(t + 1) * P, :]).then_inc(x_in, 16)
            a.dma_start(gB[0:META, :], meta_tokens).then_inc(meta_in, 16)
            for src, at in ((norm_mix_pre, V_PRE), (conv_b_in, V_BIN), (conv_b_dw, V_BDW), (conv_ln_g, V_LG),
                            (conv_ln_b, V_LB), (norm_ffn_pre, V_FPRE), (norm_mix_g_2, V_MIX2)):
                r = src.rearrange("a (k p) -> (a k) p", p=P)
                a.dma_start(vst[at:at + r.shape[0], 0, :], r).then_inc(vec_in, 16)
            taps = conv_w_dw[0].rearrange("t (k p) -> (t k) p", p=P)
            for q in range(4):
                r = min(P, TAPS * KT - q * P)
                a.dma_start(vst[0:r, 1 + q, :], taps[q * P:q * P + r, :]).then_inc(vec_in, 16)
            a.dma_start(vst[0:3 * CT, 5, :], conv_w_2[0].rearrange("t (k p) -> (t k) p", p=P)).then_inc(vec_in, 16)
            a.dma_start(wst, sgu_w_s_2[0].rearrange("h i j -> i h j")).then_inc(ws_in, 16)

            a.dma_start(wr[:, :, 0:GROUPS], w_router_group_2[0].rearrange("(k p) g -> p k g", p=P)).then_inc(wr_in, 16)
            a.dma_start(wr[:, :, GROUPS:GROUPS + EXPERTS],
                        w_router_expert_2[0].rearrange("(k p) g -> p k g", p=P)).then_inc(wr_in, 16)

            a.wait_ge(var_ready, 3)
            for t in range(TOK):
                a.wait_ge(x_in, 32)
                fn(tiles[:, 8 * t:8 * t + 8, :].rearrange("p k c -> p (k c)"), h[:, t, :], ACT.Square,
                   accum_out=st[:, SS + t:SS + t + 1]).then_inc(ssq_ready, 1)
            a.wait_ge(meta_in, 16)
            fn(tiles[0:META, 16:24, :].rearrange("p k c -> p (k c)"), gB[0:META, :], ACT.Square,
               accum_out=st[0:META, SS + 2:SS + 3]).then_inc(ssq_ready, 1)
            a.wait_ge(ssq_ready, 3)
            root(st[:, SS:SS + 3], st[:, RT:RT + 3], 1.0 / D, st[:, EPS_AT:EPS_AT + 1])

            hi(0, 0)
            hi(0, 1)

            a.wait_ge(vec_ready, 1)
            for k in range(KT):
                a.wait_ge(turned, k + 1)
                fn(xTA[:, k, 0:TM], ps[:, k % 8, 0:TM], ACT.Copy,
                   scale=vcol[:, V_PRE + k:V_PRE + k + 1]).then_inc(xhi_ready, 1)

            with a.Fori(0, KT // 2) as g:
                for s in range(4):
                    m = s // 2
                    if s % 2:
                        a.wait_ge(glu_done, g * 2 + (m + 2 - 1))
                    hi(g * 4, s + 2)
                    if s % 2:
                        fn(sgA[:, m, :], ps[:, 4 + s, 0:TM], ACT.Sigmoid,
                           bias=vcol[:, ds(g * 2 + (V_BIN + KT + m), 1)]).then_inc(sig_a, 1)

            for q in range(4):
                a.wait_ge(cent, q + 1)
                fn(tmp[:, q // 2, (q % 2) * 4 * T:(q % 2 + 1) * 4 * T],
                   cv[:, 4 * q:4 * q + 4, :].rearrange("p k c -> p (k c)"), ACT.Square).then_inc(sq_done, 1)
            a.wait_ge(sums_done, 2)
            root(ps[:, 1, 0:T], rstdb, 1.0 / D, st[:, LN_EPS_AT:LN_EPS_AT + 1])

            def silu_tile(j, s):
                a.wait_ge(z_ready, j + (s + 1))
                a.wait_ge(u_ready, j + (s - 1 + 2))
                fn(sg[:, s % 2, :], xs[:, s % 2, :], ACT.Sigmoid).then_inc(zs_ready, 1)

            def split_act(src, step, s, panel, ready=None):
                if ready is not None:
                    a.wait_ge(ready[0], ready[1])
                if panel is not None:
                    a.wait_ge(mm_done, panel - 1)
                fn(act[:, s % 2, 0, :], src, ACT.Copy).then_inc(act_hi, 1)

            def tile_of(v, j, s):
                if isinstance(j, int):
                    return v[:, j + s, :]
                return v[:, ds(j + s, 1), :].rearrange("p a c -> p (a c)")

            for s in range(4):
                if s < 2:
                    silu_tile(0, s)
                if s >= 2:
                    split_act(xs[:, s % 2, :], S_B, s - 2, B + s - 2, (u_ready, s - 1 + 2))
                    silu_tile(0, s)

            def b_group(j, last=False):
                for s in range(4):
                    hi(j + B, s + 2)
                    if not (last and s >= 2):
                        split_act(xs[:, s % 2, :], S_B, s, None, (u_ready, j + (s + 3 + 2)))
                    if not last:
                        silu_tile(j, s + 4)

            with a.Fori(0, (KT - 4) // 4) as r:
                j = r * 4
                b_group(j)
            b_group(KT - 4, last=True)

            def post(q, last_panel):
                a.wait_ge(mm_done, last_panel)
                for t in range(TOK):
                    for c in range(NC):
                        fn(tmp[:, t, c * BANK:(c + 1) * BANK], ps[:, t * NC + c, :], ACT.Square,
                           accum_out=st[:, SSQ + t * NC + c:SSQ + t * NC + c + 1]).then_inc(ssq_ready, 1)
                for t in range(TOK):
                    a.wait_ge(var_ready, 3 + 2 * q + t + 1)
                    root(st[:, SS + t:SS + t + 1], st[:, RT + t:RT + t + 1], 1.0 / D, st[:, EPS_AT:EPS_AT + 1])
                pre(3 + 10 * q + 8, 8 * (q + 1))

            def pre(ssq_at, added):
                for t in range(TOK):
                    a.wait_ge(add_done, added - 4 * (TOK - 1 - t))
                    fn(tmp[:, t, :], h[:, t, :], ACT.Square, accum_out=st[:, SS + t:SS + t + 1]).then_inc(ssq_ready, 1)
                    a.wait_ge(ssq_ready, ssq_at + t + 1)
                    root(st[:, SS + t:SS + t + 1], st[:, RT + t:RT + t + 1], 1.0 / D, st[:, EPS_AT:EPS_AT + 1])

            def turn(count, gain):
                for k in range(KT):
                    a.wait_ge(turned, KT * count + k + 1)
                    fn(xT5[:, k, 0:T], ps[:, k % 8, 0:T], ACT.Copy,
                       scale=vcol[:, gain + k:gain + k + 1]).then_inc(xhi_ready, 1)

            post(0, C)
            turn(1, V_FPRE)

            def half(f, s, bank):
                a.wait_ge(feat_free, f + (s + 4 - 1))
                fn(t1[:, s % 2, :], ps[:, bank, T:2 * T], ACT.Copy).then_inc(feat_half, 1)

            with a.Fori(0, FT // 2) as g:
                for s in range(4):
                    a.wait_ge(mm_done, g * 4 + (C + s + 1))
                    half(g * 4 + F_C, s, 4 + s)
                    hi(g * 4 + C, s + 2)
                    if s % 2:
                        a.wait_ge(feat_free, g * 4 + (F_C + s + 4))
                        a.wait_ge(hid_ready, g * 2 + (s // 2 + 2 - 1))
                        fn(sg[:, s // 2, :], xs[:, s // 2, :], ACT.Sigmoid).then_inc(sig_c, 1)

            def rows(n0, src, step, count, ready):
                def group(j, last=False):
                    for s in range(4):
                        hi(j + n0, s + 2)
                        if not (last and s >= 2):
                            split_act(tile_of(src, j, s + 2), step, s, None)
                for s in range(2):
                    split_act(src[:, s, :], step, s, n0 + s, ready)
                with a.Fori(0, (count - 4) // 4) as r:
                    j = r * 4
                    group(j)
                return group(count - 4, last=True)

            rows(DN, tiles, S_D, FT, (hid_ready, FT + 2))
            post(1, ZV)
            turn(2, V_MIX2)

            for q in range(8):
                hi(ZV, q + 2)
            for b in range(4):
                fn(vscr[:, b * BANK:(b + 1) * BANK], ps[:, b, :], ACT.Square).then_inc(vsq, 1)
            for b in range(4):
                a.wait_ge(varg, b + 1)
                fn(vscr[:, b * BANK:(b + 1) * BANK], vscr[:, b * BANK:(b + 1) * BANK], ACT.Sigmoid).then_inc(vsig, 1)
            for t in range(TOK):
                a.wait_ge(var_ready, 7 + t + 1)
                fn(st[:, RT + t:RT + t + 1], st[:, MV + 2 * t + 1:MV + 2 * t + 2], ACT.Sqrt, bias=st[:, EPS_AT:EPS_AT + 1]).then_inc(root_ready, 1)

            def halves(n0, f0, count):
                with a.Fori(0, (count) // 4) as r:
                    j = r * 4
                    for s in range(4):
                        a.wait_ge(mm_done, j + (n0 + s + 1))
                        half(j + f0, s, 4 + s)
                        hi(j + n0, s + 2)

            halves(CH, F_E, 2 * CT)
            halves(BG, F_E + BG - CH, CT)
            with a.Fori(0, (CT) // 4) as r:
                j = r * 4
                for s in range(4):
                    f = F_E + U - CH
                    a.wait_ge(mm_done, j + (U + s + 1))
                    half(j + f, s, 4 + s)
                    hi(j + U, s + 2)
                    a.wait_ge(feat_free, j + (f + s + 5))
                    fn(sg[:, s % 2, :], xs[:, s % 2, :], ACT.Square).then_inc(usq, 1)
                    a.wait_ge(uarg, j + (s + 1))
                    fn(sg[:, s % 2, :], sg[:, s % 2, :], ACT.Sigmoid).then_inc(usig, 1)
            a.sem_inc(gate_ready, 2)
            with a.Fori(0, (2 * KT) // 4) as r:
                j = r * 4
                for s in range(4):
                    f = F_E + GT - CH
                    a.wait_ge(mm_done, j + (GT + s + 1))
                    half(j + f, s, 4 + s)
                    a.wait_ge(feat_free, j + (f + s + 5))
                    hi(j + GT, s + 2)
                    fn(tile_of(tiles, j, s), xs[:, s % 2, :], ACT.Sigmoid).then_inc(gate_ready, 1)

            a.wait_ge(mm_done, UP)
            for q in range(4):
                src = yc if q < 2 else tiles[:, UT:UT + CT, :]
                k = (q % 2) * 4
                if q == 2:
                    a.wait_ge(ys_ready, CT)
                fn(xT5[:, 4 * q:4 * q + 4, 0:T], src[:, k:k + 4, :], ACT.Copy).then_inc(pair_hi, 1)

            with a.Fori(0, (2 * CT) // 4) as r:
                j = r * 4
                for s in range(4):
                    a.wait_ge(mm_done, j + (UP + s + 1))
                    for b in range(2):
                        half(j * 2 + F_UP, 2 * s + b, 4 + (2 * s + b) % 4)
                    hi(j + UP, s + 2)

            for s in range(2):
                a.wait_ge(fused_done, 1)
                fn(act[:, s, 0, :], tiles[:, s, :], ACT.Copy).then_inc(act_hi, 1)

            def g_group(j, last=False):
                for s in range(4):
                    if not (last and s >= 2):
                        hi(j + G, s + 2)
                        split_act(tile_of(tiles, j, s + 2), S_G, s, None)
            with a.Fori(0, (KT - 4) // 4) as r:
                j = r * 4
                g_group(j)
            g_group(KT - 4, last=True)

            pre(23, 24)
            for t in range(TOK):
                a.wait_ge(xn_ready, 7 + t + 1)
                fn(tH[:, t, :], tmp[:, t, :], ACT.Copy).then_inc(thi_ready, 1)
            for q in range(8):
                a.wait_ge(tt_turned, q + 1)
                fn(tiles[:, 2 * q:2 * q + 2, :].rearrange("p k c -> p (k c)"), ps[:, q, :], ACT.Copy).then_inc(tt_ready, 1)
            a.wait_ge(r_shift, 1)
            fn(st[:, 64:72], st[:, 56:64], ACT.Exp).then_inc(r_exp, 1)
            a.wait_ge(r_shift, 2)
            fn(st[:, 80:88], st[:, 72:80], ACT.Exp).then_inc(r_exp, 1)

            a.wait_ge(jobs_ready, 1)
            jobs = nc.scalar.value_load(sti[0:1, 0:1], min_val=GROUPS, max_val=GROUPS + 1)
            with a.Fori(0, jobs) as jb:
                n = jb * JOB + MOE
                a.wait_ge(slot_done, jb + 1)
                fn(SelT, ps[:, 2, 0:2 * P].rearrange("p (t c) -> p t c", t=TOK), ACT.Copy).then_inc(selT_ready, 1)
                fn(st[:, SLOTW:SLOTW + PER], ps[:, 2, 2 * P:2 * P + PER], ACT.Copy).then_inc(selT_ready, 1)
                for q in range(4):
                    a.wait_ge(gath_hi, jb * 4 + (q + 1))
                    fn(xg[:, 0, 4 * q:4 * q + 4, :].rearrange("p k c -> p (k c)"), ps[:, 4 + q, :], ACT.Copy).then_inc(xg_hi, 1)

                def gate_up(n, s0, turn_at):
                    for q in range(6):
                        hi(n, s0 + q)
                    if turn_at is not None:
                        a.wait_ge(hid_turned, turn_at)
                        fn(hT[:, 0, :, :].rearrange("p k c -> p (k c)"), ps[:, 2, :], ACT.Copy).then_inc(hT_hi, 1)
                    fn(gsl, ps[:, 0, :], ACT.Sigmoid).then_inc(sig_g, 1)
                    hi(n, s0 + 6)
                    hi(n, s0 + 7)

                gate_up(n, 0, None)
                with a.Fori(0, PER - 1) as e:
                    gate_up(n + e * 12, 8, jb * PER + e + 1)
                    for r in range(4):
                        hi(n + e * 12, 16 + r)
                hi(n, JOB - 4)
                hi(n, JOB - 3)
                a.wait_ge(hid_turned, jb * PER + PER)
                fn(hT[:, 0, :, :].rearrange("p k c -> p (k c)"), ps[:, 2, :], ACT.Copy).then_inc(hT_hi, 1)
                hi(n, JOB - 2)
                hi(n, JOB - 1)
                a.wait_ge(mm_done, n + JOB)
                for c in range(NC):
                    fn(yh[:, 0, c * BANK:(c + 1) * BANK], ps[:, 4 + c, :], ACT.Copy).then_inc(y_hi, 1)
            for t in range(TOK):
                a.wait_ge(add_done, jobs * 8 + (24 + 4 * t + 4 - 8))
                fn(tmp[:, t, :], h[:, t, :], ACT.Square, accum_out=st[:, SS + t:SS + t + 1]).then_inc(ssq_ready, 1)
                a.wait_ge(ssq_ready, 25 + t + 1)
                root(st[:, SS + t:SS + t + 1], st[:, RT + t:RT + t + 1], 1.0 / D, st[:, EPS_AT:EPS_AT + 1])

        @block.vector
        def _(v):
            own = Tally(dve_own)
            V = nc.vector

            def lo(n, s):
                v.wait_ge(hi_ready, n + (s + 1))
                V.tensor_tensor(wlo[:, s % 2, :], raw[:, s % RING, :], whi[:, s % 2, :], ALU.subtract).then_inc(lo_ready, 1)

            def flat(x3):
                return x3.rearrange("p k c -> p (k c)")

            def tile_of(t, j, s):
                if isinstance(j, int):
                    return t[:, j + s, :]
                return t[:, ds(j + s, 1), :].rearrange("p a c -> p (a c)")

            V.memset(st[:, 0:EPS_AT], 0.0).then_inc(var_ready, 1)
            V.memset(st[:, EPS_AT:EPS_AT + 1], RMS_EPS).then_inc(var_ready, 1)
            V.memset(st[:, LN_EPS_AT:LN_EPS_AT + 1], LN_EPS).then_inc(var_ready, 1)
            v.wait_ge(vec_turned, 1)
            V.tensor_copy(flat(vT[:, 0:4, :]), ps[:, 0, :])
            V.tensor_copy(vT[:, 4, 0:TAPS * KT - 3 * P], ps[:, 1, 0:TAPS * KT - 3 * P])
            V.tensor_copy(vT[:, 5, 0:3 * CT], ps[:, 1, P:P + 3 * CT]).then_inc(vec_ready, 1)
            v.wait_ge(ws_turned, 1)
            for b in range(2):
                own.mark(V.tensor_copy(flat(wsT[:, 4 * b:4 * b + 4, :]), ps[:, 2 + b, :]))
            own.wait(v)
            V.memset(wsT[HALF:P, :, 0:HALF], 0.0).then_inc(ws_ready, 1)

            v.wait_ge(root_ready, 1)
            own.mark(V.reciprocal(st[:, RS:RS + 3], st[:, RT:RT + 3]))
            own.wait(v)
            for t in range(TOK):
                V.tensor_scalar(tmp[:, t, :], h[:, t, :], st[:, RS + t:RS + t + 1], None, ALU.mult).then_inc(xn_ready, 1)
            V.tensor_scalar(gB[0:META, :], gB[0:META, :], st[0:META, RS + 2:RS + 3], None, ALU.mult).then_inc(xn_ready, 1)
            for k in range(KT):
                v.wait_ge(xhi_ready, k + 1)
                V.scalar_tensor_tensor(out=xTA[:, k, TM:2 * TM], in0=ps[:, k % 8, 0:TM],
                                       scalar=vcol[:, V_PRE + k:V_PRE + k + 1], in1=xTA[:, k, 0:TM],
                                       op0=ALU.mult, op1=ALU.subtract).then_inc(xlo_ready, 1)
            v.sem_inc(glu_done, 2)
            v.wait_ge(pad_ready, 1)

            with rounds(v, KT // 2, (own, 2 * TAPS - 2)) as g:
                for m in range(2):
                    v.wait_ge(sig_a, g * 2 + (m + 1))
                    V.scalar_tensor_tensor(out=uext[:, ds(g * 2 + m, 1), PAD:EXT].rearrange("p a c -> p (a c)"),
                                           in0=ps[:, 4 + 2 * m, 0:TM], scalar=vcol[:, ds(g * 2 + (V_BIN + m), 1)],
                                           in1=sgA[:, m, :], op0=ALU.add, op1=ALU.mult).then_inc(glu_done, 1)
                for tap in range(TAPS):
                    for m in range(2):
                        src = uext[:, ds(g * 2 + m, 1), tap:tap + T].rearrange("p a c -> p (a c)")
                        dst = cv[:, ds(g * 2 + m, 1), :].rearrange("p a c -> p (a c)")
                        w = vcol[:, ds(g * 2 + (V_DW + tap * KT + m), 1)]
                        if tap == 0:
                            v.wait_ge(glu_done, g * 2 + (m + 1 + 2))
                            ins = V.tensor_scalar(dst, src, w, vcol[:, ds(g * 2 + (V_BDW + m), 1)], ALU.mult, ALU.add)
                        else:
                            own.wait(v, 1 if tap < TAPS - 1 or m == 0 else 0)
                            ins = V.scalar_tensor_tensor(out=dst, in0=src, scalar=w, in1=dst, op0=ALU.mult, op1=ALU.add)
                        if tap == TAPS - 1:
                            ins.then_inc(conv_done, 1)
                        else:
                            own.mark(ins)
            lo(B, 0)
            lo(B, 1)

            v.wait_ge(sums_done, 1)
            own.mark(V.tensor_scalar(meanb, ps[:, 0, 0:T], 1.0 / D, None, ALU.mult))
            own.wait(v)
            for q in range(4):
                V.tensor_tensor(cv[:, 4 * q:4 * q + 4, :], cv[:, 4 * q:4 * q + 4, :],
                                meanb.rearrange("p (a c) -> p a c", a=1).to_broadcast([P, 4, T]), ALU.subtract).then_inc(cent, 1)
            v.wait_ge(root_ready, 2)
            own.mark(V.reciprocal(rstdb, rstdb))
            own.wait(v)
            v.sem_inc(u_ready, 2)

            def norm_tile(j, s):
                t = xs[:, s % 2, :]
                if not (isinstance(j, int) and j + s < 2):
                    v.wait_ge(act_lo, j + (s - 1))
                own.mark(V.tensor_tensor(t, tile_of(cv, j, s), rstdb, ALU.mult))
                own.wait(v)
                gcol = vcol[:, ds(j + (V_LG + s), 1)]
                bcol = vcol[:, ds(j + (V_LB + s), 1)]
                V.tensor_scalar(t, t, gcol, bcol, ALU.mult, ALU.add).then_inc(z_ready, 1)

            def silu_tile(j, s):
                v.wait_ge(zs_ready, j + (s + 1))
                t = xs[:, s % 2, :]
                V.tensor_tensor(t, t, sg[:, s % 2, :], ALU.mult).then_inc(u_ready, 1)

            def split_act(src, s, count):
                v.wait_ge(act_hi, count)
                V.tensor_tensor(act[:, s % 2, 1, :], src, act[:, s % 2, 0, :], ALU.subtract).then_inc(act_lo, 1)

            for s in range(4):
                if s >= 2:
                    split_act(xs[:, s % 2, :], s, S_B + s - 1)
                norm_tile(0, s)
                silu_tile(0, s)

            def b_group(j, last=False):
                for s in range(4):
                    if not (last and s >= 2):
                        split_act(xs[:, s % 2, :], s, j + (S_B + s + 3))
                    if not last:
                        norm_tile(j, s + 4)
                    lo(j + B, s + 2)
                    if not last:
                        silu_tile(j, s + 4)

            with rounds(v, (KT - 4) // 4, (own, 4)) as r:
                b_group(r * 4)
            b_group(KT - 4, last=True)

            def post(q, gain):
                for t in range(TOK):
                    v.wait_ge(ssq_ready, 3 + 10 * q + NC * (t + 1))
                    V.reduce_sum(st[:, SS + t:SS + t + 1], st[:, SSQ + NC * t:SSQ + NC * (t + 1)], AX_X).then_inc(var_ready, 1)
                for t in range(TOK):
                    v.wait_ge(root_ready, 2 + 4 * q + t + 1)
                    own.mark(V.reciprocal(st[:, RS + t:RS + t + 1], st[:, RT + t:RT + t + 1]))
                    own.wait(v)
                    v.wait_ge(gain_in, gain)
                    for c in range(NC):
                        V.scalar_tensor_tensor(out=tmp[:, t, c * BANK:(c + 1) * BANK], in0=ps[:, t * NC + c, :],
                                               scalar=st[:, RS + t:RS + t + 1], in1=gB[:, c * BANK:(c + 1) * BANK],
                                               op0=ALU.mult, op1=ALU.mult).then_inc(post_done, 1)
                    v.wait_ge(post_done, 8 * q + NC * (t + 1))
                    V.tensor_tensor(h[:, t, :], h[:, t, :], tmp[:, t, :], ALU.add).then_inc(add_done, 4)
                pre(3 + 10 * q + 8, 2 + 4 * q + 2)

            def pre(ssq_at, root_at, gain=None):
                for t in range(TOK):
                    v.wait_ge(ssq_ready, ssq_at + t + 1)
                    v.wait_ge(root_ready, root_at + t + 1)
                    own.mark(V.reciprocal(st[:, RS + t:RS + t + 1], st[:, RT + t:RT + t + 1]))
                    own.wait(v)
                    if gain is None:
                        V.tensor_scalar(tmp[:, t, :], h[:, t, :], st[:, RS + t:RS + t + 1], None, ALU.mult).then_inc(xn_ready, 1)
                    else:
                        v.wait_ge(gain_in, gain)
                        V.scalar_tensor_tensor(out=tmp[:, t, :], in0=h[:, t, :], scalar=st[:, RS + t:RS + t + 1],
                                               in1=gB[:, :], op0=ALU.mult, op1=ALU.mult).then_inc(xn_ready, 1)

            def turn(count, gain):
                for k in range(KT):
                    v.wait_ge(xhi_ready, KT * count + k + 1)
                    V.scalar_tensor_tensor(out=xT5[:, k, T:2 * T], in0=ps[:, k % 8, 0:T],
                                           scalar=vcol[:, gain + k:gain + k + 1], in1=xT5[:, k, 0:T],
                                           op0=ALU.mult, op1=ALU.subtract).then_inc(xlo_ready, 1)

            post(0, 32)
            v.sem_inc(feat_free, 4)
            v.sem_inc(hid_ready, 2)
            turn(1, V_FPRE)

            def joined(f, s, bank, dst):
                v.wait_ge(feat_half, f + (s + 1))
                V.tensor_tensor(dst, ps[:, bank, 0:T], t1[:, s % 2, :], ALU.add).then_inc(feat_free, 1)

            with rounds(v, FT // 2, (own, 2)) as g:
                for s in range(4):
                    if s % 2:
                        v.wait_ge(hid_ready, g * 2 + (s // 2 + 2))
                    joined(g * 4 + F_C, s, 4 + s, xs[:, 2 if s % 2 else s // 2, :])
                    lo(g * 4 + C, s + 2)
                    if s % 2:
                        v.wait_ge(sig_c, g * 2 + (s // 2 + 1))
                        own.mark(V.tensor_tensor(sg[:, s // 2, :], sg[:, s // 2, :], xs[:, s // 2, :], ALU.mult))
                        own.wait(v)
                        v.wait_ge(feat_free, g * 4 + (F_C + s + 5))
                        V.tensor_tensor(tile_of(tiles, g * 2, s // 2), sg[:, s // 2, :], xs[:, 2, :], ALU.mult).then_inc(hid_ready, 1)

            def rows(n0, src, step, count):
                def group(j, last=False):
                    for s in range(4):
                        if not (last and s >= 2):
                            split_act(tile_of(src, j, s + 2), s, j + (step + s + 3))
                        lo(j + n0, s + 2)
                for s in range(2):
                    split_act(src[:, s, :], s, step + s + 1)
                with v.Fori(0, (count - 4) // 4) as r:
                    j = r * 4
                    group(j)
                group(count - 4, last=True)

            rows(DN, tiles, S_D, FT)
            post(1, 48)
            turn(2, V_MIX2)

            for q in range(8):
                lo(ZV, q + 2)
            for b in range(4):
                v.wait_ge(vsq, b + 1)
                t = vscr[:, b * BANK:(b + 1) * BANK]
                own.mark(V.tensor_scalar(t, t, GELU_B, GELU_A, ALU.mult, ALU.add))
                own.wait(v)
                V.tensor_tensor(t, t, ps[:, b, :], ALU.mult).then_inc(varg, 1)
            for b in range(4):
                v.wait_ge(vsig, b + 1)
                V.tensor_tensor(vbuf[:, b // 2, (b % 2) * BANK:(b % 2 + 1) * BANK],
                                vscr[:, b * BANK:(b + 1) * BANK], ps[:, b, :], ALU.mult).then_inc(v_free, 1)
            for t in range(TOK):
                v.wait_ge(v_free, 2 * t + 2)
                for c in range(2):
                    own.mark(V.bn_stats(st[:, BN + 12 * t + 6 * c:BN + 12 * t + 6 * c + 6], vbuf[:, t, c * BANK:(c + 1) * BANK]))
                own.wait(v)
                V.bn_aggr(st[:, MV + 2 * t:MV + 2 * t + 2], st[:, BN + 12 * t:BN + 12 * t + 12].rearrange("p (a c) -> p a c", a=2)).then_inc(var_ready, 1)
                v.wait_ge(root_ready, 10 + t + 1)
                own.mark(V.reciprocal(st[:, RS + t:RS + t + 1], st[:, RT + t:RT + t + 1]))
                own.wait(v)
                V.tensor_scalar(vbuf[:, t, :], vbuf[:, t, :], st[:, MV + 2 * t:MV + 2 * t + 1],
                                st[:, RS + t:RS + t + 1], ALU.subtract, ALU.mult).then_inc(v_norm, 1)

            own.mark(V.memset(pext[:, :, 0:2], 0.0))
            own.wait(v)
            with rounds(v, CT // 2, (own, 8)) as g:
                for s in range(4):
                    m = s // 2
                    joined(g * 4 + F_E, s, 4 + s, xs[:, 2 if s % 2 else m, :])
                    lo(g * 4 + CH, s + 2)
                    if s % 2:
                        v.wait_ge(feat_free, g * 4 + (F_E + s + 5))
                        own.mark(V.tensor_tensor(pext[:, m, 2:T + 2], xs[:, m, :], xs[:, 2, :], ALU.mult))
                        own.wait(v)
                        y = tile_of(yc, g * 2, m)

                        def w(tap):
                            return vcol[:, ds(g * 2 + (V_CW2 + tap * CT + m), 1)]
                        own.mark(V.tensor_scalar(y, pext[:, m, 0:T], w(0), None, ALU.mult))
                        for tap in (1, 2):
                            own.wait(v)
                            own.mark(V.scalar_tensor_tensor(out=y, in0=pext[:, m, tap:tap + T], scalar=w(tap), in1=y,
                                                            op0=ALU.mult, op1=ALU.add))
            own.wait(v)
            with rounds(v, CT // 4, (own, 4)) as r:
                for s in range(4):
                    f = F_E + BG - CH
                    own.wait(v, 1)
                    joined(r * 4 + f, s, 4 + s, xs[:, s % 2, :])
                    lo(r * 4 + BG, s + 2)
                    v.wait_ge(feat_free, r * 4 + (f + s + 5))
                    y = tile_of(yc, r * 4, s)
                    own.mark(V.tensor_tensor(y, y, xs[:, s % 2, :], ALU.mult))
            v.wait_ge(spat_done, 1)
            v.wait_ge(bs_in, 16)
            for b in range(4):
                V.tensor_tensor(vmb[:, b * BANK:(b + 1) * BANK].rearrange("p (h n i) -> p h n i", h=2, n=TOK),
                                ps[:, b, :].rearrange("p (h n i) -> p h n i", h=2, n=TOK),
                                bsB[:, 2 * b:2 * b + 2, :].rearrange("p h (a i) -> p h a i", a=1).to_broadcast([P, 2, TOK, P]),
                                ALU.add).then_inc(vm_ready, 1)
            v.sem_inc(ut_ready, 2)
            own.wait(v)
            with rounds(v, CT // 4, (own, 4)) as r:
                for s in range(4):
                    f = F_E + U - CH
                    v.wait_ge(ut_ready, r * 4 + (s - 1 + 2))
                    joined(r * 4 + f, s, 4 + s, xs[:, s % 2, :])
                    lo(r * 4 + U, s + 2)
                    v.wait_ge(usq, r * 4 + (s + 1))
                    t = sg[:, s % 2, :]
                    own.mark(V.tensor_scalar(t, t, GELU_B, GELU_A, ALU.mult, ALU.add))
                    own.wait(v)
                    V.tensor_tensor(t, t, xs[:, s % 2, :], ALU.mult).then_inc(uarg, 1)
                    v.wait_ge(usig, r * 4 + (s + 1))
                    V.tensor_tensor(tile_of(tiles, r * 4 + UT, s), t, xs[:, s % 2, :], ALU.mult).then_inc(ut_ready, 1)
            v.wait_ge(ut_ready, CT + 2)
            with v.Fori(0, (2 * KT) // 4) as r:
                j = r * 4
                for s in range(4):
                    f = F_E + GT - CH
                    v.wait_ge(gate_ready, j + (s - 1 + 2))
                    joined(j + f, s, 4 + s, xs[:, s % 2, :])
                    lo(j + GT, s + 2)

            own.wait(v)
            for q in range(4):
                src = yc if q < 2 else tiles[:, UT:UT + CT, :]
                k = (q % 2) * 4
                v.wait_ge(pair_hi, q + 1)
                V.tensor_tensor(xT5[:, 4 * q:4 * q + 4, T:2 * T], src[:, k:k + 4, :], xT5[:, 4 * q:4 * q + 4, 0:T],
                                ALU.subtract).then_inc(pair_lo, 1)

            v.wait_ge(gate_ready, 2 * KT + 2)
            with rounds(v, CT // 2, (own, 16 - 4)) as r:
                for s in range(4):
                    for b in range(2):
                        i = 2 * s + b
                        m, br = 2 * (s // 2) + b, s % 2
                        own.wait(v)
                        joined(r * 8 + F_UP, i, 4 + i % 4, xs[:, b, :])
                        v.wait_ge(feat_free, r * 8 + (F_UP + i + 5))
                        gate = tile_of(tiles, r * 4 + br * KT, m)
                        own.mark(V.tensor_tensor(gate, gate, xs[:, b, :], ALU.mult))
                        if br:
                            own.wait(v)
                            own.mark(V.tensor_tensor(tile_of(tiles, r * 4, m), tile_of(tiles, r * 4, m), gate, ALU.add))
                    lo(r * 4 + UP, s + 2)
            own.wait(v)
            v.sem_inc(fused_done, 1)

            def g_rows():
                def group(j, last=False):
                    for s in range(4):
                        if not (last and s >= 2):
                            split_act(tile_of(tiles, j, s + 2), s, j + (S_G + s + 3))
                            lo(j + G, s + 2)
                for s in range(2):
                    split_act(tiles[:, s, :], s, S_G + s + 1)
                with v.Fori(0, (KT - 4) // 4) as r:
                    j = r * 4
                    group(j)
                group(KT - 4, last=True)
            g_rows()

            v.wait_ge(mm_done, MOE)
            for t in range(TOK):
                for c in range(NC):
                    hc = h[:, t, c * BANK:(c + 1) * BANK]
                    V.tensor_tensor(hc, hc, ps[:, t * NC + c, :], ALU.add).then_inc(add_done, 1)
            pre(23, 12, gain=96)
            for t in range(TOK):
                v.wait_ge(thi_ready, t + 1)
                V.tensor_tensor(tL[:, t, :], tmp[:, t, :], tH[:, t, :], ALU.subtract).then_inc(tlo_ready, 1)

            R = wk[:, 0:512]
            at = [0]

            def cols(n, shape=None):
                r = R[:, at[0]:at[0] + n]
                at[0] += n
                return r

            def step(ins):
                own.mark(ins)
                own.wait(v)

            NL = GROUPS + EXPERTS
            lg = cols(TOK * NL).rearrange("p (t c) -> p t c", t=TOK)
            mx = cols(2)
            pri = cols(8).rearrange("p (t c) -> p t c", t=TOK)
            eq = cols(8).rearrange("p (t c) -> p t c", t=TOK)
            ohg = cols(8).rearrange("p (t c) -> p t c", t=TOK)
            oh1 = cols(8).rearrange("p (t c) -> p t c", t=TOK)
            oh2 = cols(8).rearrange("p (t c) -> p t c", t=TOK)
            sel = cols(8).rearrange("p (t c) -> p t c", t=TOK)
            gate = cols(8).rearrange("p (t c) -> p t c", t=TOK)
            pg = cols(2)
            zz = cols(2)
            rank = cols(2)
            inlow = cols(2)
            slot = cols(TOK * (GROUPS + 1)).rearrange("p (t c) -> p t c", t=TOK)
            ovf = cols(4)
            num = cols(4)
            jf = cols(2)
            assert at[0] <= 512 and OHG == TOK * NL + 2 + 16 and GATE == OHG + 32
            dg = st[:, 56:64].rearrange("p (t c) -> p t c", t=TOK)
            eg = st[:, 64:72].rearrange("p (t c) -> p t c", t=TOK)
            d1 = st[:, 72:80].rearrange("p (t c) -> p t c", t=TOK)
            e1 = st[:, 80:88].rearrange("p (t c) -> p t c", t=TOK)

            def bc(x2, n):
                return x2.rearrange("p (t a) -> p t a", a=1).to_broadcast([P, TOK, n])

            for i in range(GROUPS):
                V.memset(pri[:, :, i], float(GROUPS - i))
                V.memset(num[:, i:i + 1], float(i))

            def first_max(oh, d):
                step(V.tensor_scalar(eq, d, 0.0, None, ALU.is_equal))
                step(V.tensor_tensor(eq, eq, pri, ALU.mult))
                step(V.reduce_max(mx, eq, AX_X))
                step(V.tensor_tensor(oh, eq, bc(mx, 4), ALU.is_equal))

            v.wait_ge(logits_done, 1)
            step(V.tensor_copy(lg, ps[:, 0, 0:2 * 32].rearrange("p (t c) -> p t c", t=2)[:, :, 0:NL]))
            step(V.reduce_max(mx, lg[:, :, 0:GROUPS], AX_X))
            V.tensor_tensor(dg, lg[:, :, 0:GROUPS], bc(mx, 4), ALU.subtract).then_inc(r_shift, 1)
            v.wait_ge(r_shift, 1)
            first_max(ohg, dg)
            v.sem_inc(r_mask, 1)
            for t in range(TOK):
                step(V.tensor_scalar(sel[:, t, :], lg[:, t, GROUPS:GROUPS + PER], ohg[:, t, 0:1], None, ALU.mult))
                for g in range(1, GROUPS):
                    step(V.scalar_tensor_tensor(out=sel[:, t, :], in0=lg[:, t, GROUPS + PER * g:GROUPS + PER * (g + 1)],
                                                scalar=ohg[:, t, g:g + 1], in1=sel[:, t, :], op0=ALU.mult, op1=ALU.add))
            step(V.reduce_max(mx, sel, AX_X))
            V.tensor_tensor(d1, sel, bc(mx, 4), ALU.subtract).then_inc(r_shift, 1)
            v.wait_ge(r_shift, 2)
            first_max(oh1, d1)
            step(V.scalar_tensor_tensor(out=sel, in0=oh1, scalar=-1e30, in1=d1, op0=ALU.mult, op1=ALU.add))
            step(V.reduce_max(mx, sel, AX_X))
            step(V.tensor_tensor(sel, sel, bc(mx, 4), ALU.subtract))
            first_max(oh2, sel)
            step(V.tensor_tensor(oh1, oh1, oh2, ALU.add))
            v.wait_ge(r_exp, 2)
            step(V.tensor_tensor(gate, oh1, e1, ALU.mult))
            step(V.reduce_sum(zz, gate, AX_X))
            step(V.reduce_sum(pg, eg, AX_X))
            step(V.tensor_tensor(zz, zz, pg, ALU.mult))
            step(V.reciprocal(zz, zz))
            step(V.tensor_tensor(gate, gate, bc(zz, 4), ALU.mult))
            v.wait_ge(rank_done, 1)
            rk = ps[:, 1, 0:8].rearrange("p (t c) -> p t c", t=TOK)
            step(V.tensor_tensor(eq, ohg, rk, ALU.mult))
            step(V.reduce_sum(rank, eq, AX_X))
            step(V.tensor_scalar(inlow, rank, float(P), None, ALU.is_lt))
            step(V.tensor_scalar(rank, rank, 1.0, None, ALU.add))
            step(V.tensor_tensor(mx, inlow, rank, ALU.mult))
            step(V.tensor_tensor(slot[:, :, 0:GROUPS], ohg, bc(mx, GROUPS), ALU.mult))
            step(V.tensor_tensor(mx, rank, mx, ALU.subtract))
            step(V.tensor_scalar(zz, inlow, float(P), float(-P), ALU.mult, ALU.add))
            step(V.tensor_tensor(slot[:, :, GROUPS], mx, zz, ALU.add))
            step(V.tensor_scalar(slot, slot, -1.0, None, ALU.add))
            step(V.tensor_scalar(ovf, ps[:, 1, 8:12], float(P), None, ALU.is_gt))
            step(V.reduce_sum(jf[:, 0:1], ovf, AX_X))
            step(V.tensor_scalar(jf[:, 0:1], jf[:, 0:1], float(GROUPS), None, ALU.add))
            step(V.tensor_tensor(ovf, ovf, num, ALU.mult))
            step(V.reduce_sum(jf[:, 1:2], ovf, AX_X))
            V.tensor_copy(sti[:, :], jf).then_inc(jobs_ready, 1)
            v.wait_ge(jobs_ready, 1)
            v.wait_ge(tri_ready, 2)
            step(V.tensor_copy(iota, iota.bitcast(I32)))
            gates = gate

            jobs = nc.vector.value_load(sti[0:1, 0:1], min_val=GROUPS, max_val=GROUPS + 1)
            with v.Fori(0, jobs) as jb:
                n = jb * JOB + MOE
                for t in range(TOK):
                    V.tensor_scalar(Sel[:, t, :], iota, slot[:, t, ds(jb, 1)], None, ALU.is_equal).then_inc(sel_ready, 1)
                for q in range(4):
                    v.wait_ge(gath_lo, jb * 4 + (q + 1))
                    V.tensor_copy(flat(xg[:, 1, 4 * q:4 * q + 4, :]), ps[:, (0, 1, 3, 2)[q], :]).then_inc(xg_lo, 1)

                def turned_lo(count):
                    v.wait_ge(hT_hi, count)
                    V.tensor_tensor(flat(hT[:, 1, :, :]), ps[:, 2, :], flat(hT[:, 0, :, :]), ALU.subtract).then_inc(hT_lo, 1)

                def gate_up(n, s0, count, turn_at):
                    for q in range(6):
                        lo(n, s0 + q)
                    if turn_at is not None:
                        turned_lo(turn_at)
                    v.wait_ge(sig_g, count)
                    V.tensor_tensor(gsl, gsl, ps[:, 0, :], ALU.mult).then_inc(gsl_ready, 1)
                    lo(n, s0 + 6)
                    lo(n, s0 + 7)

                def hidden(n, last, e, count):
                    v.wait_ge(mm_done, n + last)
                    v.wait_ge(gsl_ready, count)
                    V.scalar_tensor_tensor(out=hid, in0=ps[:, 1, :], scalar=st[:, ds(e, 1)],
                                           in1=gsl, op0=ALU.mult, op1=ALU.mult).then_inc(hid_e, 1)

                gate_up(n, 0, jb * PER + 1, None)
                v.wait_ge(selT_ready, jb * 2 + 2)
                hidden(n, 8, SLOTW, jb * PER + 1)
                with v.Fori(0, PER - 1) as e:
                    gate_up(n + e * 12, 8, jb * PER + e + 2, jb * PER + e + 1)
                    lo(n + e * 12, 16)
                    lo(n + e * 12, 17)
                    hidden(n + e * 12, 16, e + (SLOTW + 1), jb * PER + e + 2)
                    lo(n + e * 12, 18)
                    lo(n + e * 12, 19)
                lo(n, JOB - 4)
                lo(n, JOB - 3)
                turned_lo(jb * PER + PER)
                lo(n, JOB - 2)
                lo(n, JOB - 1)
                for c in range(NC):
                    v.wait_ge(y_hi, jb * 4 + (c + 1))
                    V.tensor_tensor(yh[:, 1, c * BANK:(c + 1) * BANK], ps[:, 4 + c, :], yh[:, 0, c * BANK:(c + 1) * BANK],
                                    ALU.subtract).then_inc(y_lo, 1)
                for t in range(TOK):
                    for c in range(NC):
                        v.wait_ge(scat_done, jb * 8 + (NC * t + c + 1))
                        hc = h[:, t, c * BANK:(c + 1) * BANK]
                        V.tensor_tensor(hc, hc, ps[:, t * NC + c, :], ALU.add).then_inc(add_done, 1)
            for t in range(TOK):
                v.wait_ge(root_ready, 14 + t + 1)
                own.mark(V.reciprocal(st[:, RS + t:RS + t + 1], st[:, RT + t:RT + t + 1]))
                own.wait(v)
                v.wait_ge(gain_in, 112)
                V.scalar_tensor_tensor(out=tmp[:, t, :], in0=h[:, t, :], scalar=st[:, RS + t:RS + t + 1],
                                       in1=gB[:, :], op0=ALU.mult, op1=ALU.mult).then_inc(fin_ready, 1)

        @block.tensor
        def _(pe):
            mm = nc.tensor.matmul
            tr = nc.tensor.transpose

            pe.wait_ge(ident_ready, 1)
            pe.wait_ge(ones_ready, 2)
            pe.wait_ge(vec_in, 16 * 12)
            for r in range(6):
                rows_in = P if r < 4 else (TAPS * KT - 3 * P if r == 4 else 3 * CT)
                t = tr(ps[:, r // 4, (r % 4) * P:(r % 4) * P + rows_in], vst[0:rows_in, r, :], ident[0:rows_in, 0:rows_in])
            t.then_inc(vec_turned, 1)
            pe.wait_ge(ws_in, 16)
            for hd in range(HEADS):
                t = tr(ps[:, 2 + hd // 4, (hd % 4) * P:(hd % 4 + 1) * P], wst[:, hd, :], ident[:, :])
            t.then_inc(ws_turned, 1)

            pe.wait_ge(xn_ready, 3)
            pe.wait_ge(vec_ready, 1)
            pe.wait_ge(ws_ready, 1)
            for k in range(KT):
                if k >= 8:
                    pe.wait_ge(xlo_ready, k - 7)
                b = ps[:, k % 8, :]
                tr(b[:, 0:META], gB[0:META, k * P:(k + 1) * P], ident[0:META, 0:META])
                for t in range(TOK):
                    i = tr(b[:, META + t * P:META + (t + 1) * P], tmp[:, t, k * P:(k + 1) * P], ident[:, :])
                i.then_inc(turned, 1)

            def sums(first, count, bank, src):
                for k in range(count):
                    i = mm(ps[:, bank, 0:T], ones[:, :], src(first, k), start=False, stop=True, skip_group_check=True)
                return i

            def open_bank(bank, width=BANK):
                return mm(ps[:, bank, 0:width], zrow[:, 0:P], zrow[:, 0:width], start=True, stop=True)

            pe.wait_ge(xlo_ready, KT)

            def a_group(g, first=False):
                for s in range(4):
                    bank = 4 + s
                    if not first:
                        pe.wait_ge(glu_done, g * 2 + (s // 2 - 2 + 1 + 2))
                    pe.wait_ge(hi_ready, g * 4 + (s + 1))
                    for k in range(KT):
                        w = whi[:, s % 2, k * P:(k + 1) * P]
                        mm(ps[:, bank, 0:TM], w, xTA[:, k, 0:TM], start=(k == 0), stop=False)
                        mm(ps[:, bank, 0:TM], w, xTA[:, k, TM:2 * TM], start=False, stop=False)
                    pe.wait_ge(lo_pool, g * 4 + (s + 1))
                    for k in range(KT):
                        i = mm(ps[:, bank, 0:TM], wlo[:, s % 2, k * P:(k + 1) * P], xTA[:, k, 0:TM],
                               start=False, stop=(k == KT - 1))
                    i.then_inc(mm_done, 1)
                if not first:
                    conv_sums(g, -2)

            def conv_sums(g, at):
                pe.wait_ge(conv_done, g * 2 + (at + 2))
                for m in range(2):
                    src = cv[:, ds(g * 2 + (at + m), 1), :].rearrange("p a c -> p (a c)")
                    i = mm(ps[:, 0, 0:T], ones[:, :], src, start=False, stop=True, skip_group_check=True)
                return i

            a_group(0, first=True)
            open_bank(0, T)
            open_bank(1, T)
            with pe.Fori(1, KT // 2) as g:
                a_group(g)
            conv_sums(KT // 2, -2).then_inc(sums_done, 1)
            for q in range(4):
                pe.wait_ge(sq_done, q + 1)
                for k in range(4):
                    at = (q % 2) * 4 * T + k * T
                    i = mm(ps[:, 1, 0:T], ones[:, :], tmp[:, q // 2, at:at + T], start=False, stop=True, skip_group_check=True)
            i.then_inc(sums_done, 1)

            pe.wait_ge(gain_in, 16)
            pe.wait_ge(root_ready, 2)
            pe.wait_ge(glu_done, KT + 2)
            for t in range(TOK):
                for c in range(NC):
                    i = mm(ps[:, t * NC + c, :], ones[0:1, :], gB[0:1, c * BANK:(c + 1) * BANK], start=True, stop=True)
            i.then_inc(open_done, 1)

            def row_panel(n, s, step):
                pe.wait_ge(hi_ready, n + (s + 1))
                pe.wait_ge(act_hi, step)

                def all_banks(part, w):
                    for t in range(TOK):
                        for c in range(NC):
                            i = mm(ps[:, t * NC + c, :], act[:, s % 2, part, t * P:(t + 1) * P],
                                   w[:, s % 2, c * BANK:(c + 1) * BANK], start=False, stop=True, skip_group_check=True)
                    return i
                all_banks(0, whi)
                pe.wait_ge(act_lo, step)
                all_banks(1, whi)
                pe.wait_ge(lo_ready, n + (s + 1 - B))
                all_banks(0, wlo).then_inc(mm_done, 1)

            def row_stage(n0, step, count):
                with pe.Fori(0, (count) // 4) as r:
                    j = r * 4
                    for s in range(4):
                        row_panel(j + n0, s, j + (step + s + 1))

            row_stage(B, S_B, KT)

            def turn(count):
                for k in range(KT):
                    if k == 0:
                        pe.wait_ge(xn_ready, 3 + 2 * count)
                    if k >= 8:
                        pe.wait_ge(xlo_ready, KT * count + k - 7)
                    for t in range(TOK):
                        i = tr(ps[:, k % 8, t * P:(t + 1) * P], tmp[:, t, k * P:(k + 1) * P], ident[:, :])
                    i.then_inc(turned, 1)
                pe.wait_ge(xlo_ready, KT * (count + 1))

            def feature_panel(n, s, f, bank, k0=0, count=KT, part=0, width=P):
                pe.wait_ge(feat_free, f)
                if part == 0:
                    pe.wait_ge(hi_ready, n + (s + 1))
                for k in range(count):
                    at = k * width + part * P
                    mm(ps[:, bank, :], whi[:, s % 2, at:at + P], xT5[:, k0 + k, :], start=(k == 0), stop=False)
                if part == 0:
                    pe.wait_ge(lo_ready, n + (s + 1 - B))
                for k in range(count):
                    at = k * width + part * P
                    i = mm(ps[:, bank, 0:T], wlo[:, s % 2, at:at + P], xT5[:, k0 + k, 0:T],
                           start=False, stop=(k == count - 1))
                return i

            def feature_stage(n0, f0, count):
                with pe.Fori(0, (count) // 4) as r:
                    j = r * 4
                    for s in range(4):
                        feature_panel(j + n0, s, j + (f0 + s + 1), 4 + s).then_inc(mm_done, 1)

            turn(1)
            feature_stage(C, F_C, 2 * FT)
            pe.wait_ge(feat_free, F_E + 4)
            for b in range(8):
                open_bank(b)
            row_stage(DN, S_D, FT)
            turn(2)

            for b in range(4):
                open_bank(b)
            for q in range(8):
                def banks(o, w):
                    for t in range(TOK):
                        for c in range(2):
                            for k in range(2):
                                i = mm(ps[:, 2 * t + c, :], xT5[:, 2 * q + k, o * T + t * P:o * T + (t + 1) * P],
                                       w[:, q % 2, k * SW + c * BANK:k * SW + (c + 1) * BANK],
                                       start=False, stop=True, skip_group_check=True)
                    return i
                pe.wait_ge(hi_ready, ZV + q + 1)
                banks(0, whi)
                banks(1, whi)
                pe.wait_ge(lo_ready, ZV + q + 1 - B)
                banks(0, wlo).then_inc(mm_done, 1)
            feature_stage(CH, F_E, 2 * CT)
            feature_stage(BG, F_E + BG - CH, CT)
            pe.wait_ge(v_ready, 2)
            pe.wait_ge(v_free, 4)
            for hd in range(HEADS):
                for t in range(TOK):
                    at = (hd % 2) * T + t * P
                    i = mm(ps[:, hd // 2, at:at + P], vbuf[:, t, hd * P:(hd + 1) * P], wsT[:, hd, :], start=True, stop=True)
            i.then_inc(spat_done, 1)
            feature_stage(U, F_E + U - CH, CT)
            feature_stage(GT, F_E + GT - CH, 2 * KT)
            pe.wait_ge(pair_lo, 4)
            with pe.Fori(0, (2 * CT) // 4) as r:
                j = r * 4
                for s in range(4):
                    for b in range(2):
                        i = feature_panel(j + UP, s, j * 2 + (F_UP + 2 * s + b + 1), 4 + (2 * s + b) % 4,
                                          k0=(s % 2) * CT, count=CT, part=b, width=2 * P)
                    i.then_inc(mm_done, 1)
            pe.wait_ge(feat_free, F_END + 4)
            pe.wait_ge(vm_ready, 4)
            for b in range(8):
                open_bank(b)
            row_stage(G, S_G, KT)

            pe.wait_ge(xn_ready, 7 + 2)
            for q in range(8):
                for k in range(2):
                    for t in range(TOK):
                        i = tr(ps[:, q, k * T + t * P:k * T + (t + 1) * P], tmp[:, t, (2 * q + k) * P:(2 * q + k + 1) * P], ident[:, :])
                i.then_inc(tt_turned, 1)
            pe.wait_ge(tt_ready, 8)
            pe.wait_ge(wr_in, 32)
            pe.wait_ge(bias_in, 32)
            NL = GROUPS + EXPERTS
            for t in range(TOK):
                o = ps[:, 0, 32 * t:32 * t + NL]
                mm(o, ones[0:1, :], brow[0:1, :], start=True, stop=False)
                for k in range(KT):
                    i = mm(o, tiles[:, k, t * P:(t + 1) * P], wr[:, k, :], start=False, stop=(k == KT - 1))
            i.then_inc(logits_done, 1)
            pe.wait_ge(tri_ready, 1)
            pe.wait_ge(r_mask, 1)
            ohg = wk[:, OHG:OHG + 8]
            tri = wsT[:, 0, :]
            mm(ps[:, 1, 0:4], tri, ohg[:, 0:4], start=True, stop=True)
            mm(ps[:, 1, 4:8], ones[:, :], ohg[:, 0:4], start=True, stop=False)
            mm(ps[:, 1, 4:8], tri, ohg[:, 4:8], start=False, stop=True)
            mm(ps[:, 1, 8:12], ones[:, :], ohg[:, 0:4], start=True, stop=False)
            mm(ps[:, 1, 8:12], ones[:, :], ohg[:, 4:8], start=False, stop=True).then_inc(rank_done, 1)

            pe.wait_ge(jobs_ready, 1)
            pe.wait_ge(tlo_ready, 2)
            jobs = nc.tensor.value_load(sti[0:1, 0:1], min_val=GROUPS, max_val=GROUPS + 1)
            gates = wk[:, GATE:GATE + 8]
            with pe.Fori(0, jobs) as jb:
                n = jb * JOB + MOE
                pe.wait_ge(sel_ready, jb * 2 + 2)
                pe.wait_ge(add_done, jb * 8 + 24)
                for t in range(TOK):
                    tr(ps[:, 2, t * P:(t + 1) * P], Sel[:, t, :].bitcast(F32), ident[:, :])
                for t in range(TOK):
                    i = mm(ps[:, 2, 2 * P:2 * P + PER], Sel[:, t, :].bitcast(F32), gates[:, 4 * t:4 * t + 4],
                           start=(t == 0), stop=(t == TOK - 1))
                i.then_inc(slot_done, 1)
                for part, src, order in ((0, tH, (4, 5, 6, 7)), (1, tL, (0, 1, 3, 2))):
                    for q in range(4):
                        if part and q == 3:
                            pe.wait_ge(selT_ready, jb * 2 + 2)
                        for kk in range(4):
                            k = 4 * q + kk
                            for t in range(TOK):
                                i = mm(ps[:, order[q], kk * P:(kk + 1) * P], src[:, t, k * P:(k + 1) * P], Sel[:, t, :],
                                       start=(t == 0), stop=(t == TOK - 1))
                        i.then_inc((gath_hi, gath_lo)[part], 1)
                pe.wait_ge(xg_hi, jb * 4 + 4)
                for b in range(4, 8):
                    open_bank(b)
                pe.wait_ge(xg_lo, jb * 4 + 4)

                def expert_in(n, s0, bank):
                    for q in range(4):
                        s = s0 + q
                        pe.wait_ge(hi_ready, n + (s + 1))
                        for o in range(2):
                            for k in range(4):
                                mm(ps[:, bank, :], xg[:, o, 4 * q + k, :], whi[:, s % 2, k * DE:(k + 1) * DE],
                                   start=(q == 0 and o == 0 and k == 0), stop=False)
                        pe.wait_ge(lo_ready, n + (s + 1 - B))
                        for k in range(4):
                            i = mm(ps[:, bank, :], xg[:, 0, 4 * q + k, :], wlo[:, s % 2, k * DE:(k + 1) * DE],
                                   start=False, stop=(q == 3 and k == 3))
                        i.then_inc(mm_done, 1)

                def expert_down(n, s0):
                    for r in range(ET):
                        s = s0 + r

                        def banks(o, w):
                            for c in range(NC):
                                i = mm(ps[:, 4 + c, :], hT[:, o, r, :], w[:, s % 2, c * BANK:(c + 1) * BANK],
                                       start=False, stop=True, skip_group_check=True)
                            return i
                        pe.wait_ge(hi_ready, n + (s + 1))
                        banks(0, whi)
                        banks(1, whi)
                        pe.wait_ge(lo_ready, n + (s + 1 - B))
                        banks(0, wlo).then_inc(mm_done, 1)

                def turn_hidden(count):
                    pe.wait_ge(hid_e, count)
                    for k in range(ET):
                        i = tr(ps[:, 2, k * P:(k + 1) * P], hid[:, k * P:(k + 1) * P], ident[:, :])
                    i.then_inc(hid_turned, 1)

                expert_in(n, 0, 0)
                expert_in(n, 4, 1)
                with pe.Fori(0, PER - 1) as e:
                    pe.wait_ge(gsl_ready, jb * PER + e + 1)
                    expert_in(n + e * 12, 8, 0)
                    turn_hidden(jb * PER + e + 1)
                    expert_in(n + e * 12, 12, 1)
                    pe.wait_ge(hT_lo, jb * PER + e + 1)
                    expert_down(n + e * 12, 16)
                turn_hidden(jb * PER + PER)
                pe.wait_ge(hT_lo, jb * PER + PER)
                expert_down(n, JOB - 4)
                for t in range(TOK):
                    for c in range(NC):
                        pe.wait_ge(y_lo, jb * 4 + (c + 1 if t == 0 else 4))
                        mm(ps[:, t * NC + c, :], SelT[:, t, :], yh[:, 0, c * BANK:(c + 1) * BANK], start=True, stop=False)
                        mm(ps[:, t * NC + c, :], SelT[:, t, :], yh[:, 1, c * BANK:(c + 1) * BANK],
                           start=False, stop=True).then_inc(scat_done, 1)


_INS = ['x', 'meta_tokens', 'conv_w_in', 'conv_b_in', 'conv_w_dw', 'conv_b_dw', 'conv_ln_g', 'conv_ln_b',
        'conv_w_out', 'conv_b_out', 'norm_mix_pre', 'norm_mix_post', 'norm_ffn_pre', 'norm_ffn_post',
        'ffn_w_gate', 'ffn_w_up', 'ffn_w_down', 'norm_mix_g_2', 'w_in_2', 'conv_w_2', 'sgu_ln_g_2', 'sgu_ln_b_2',
        'sgu_w_s_2', 'sgu_b_s_2', 'w_up_conv_2', 'w_up_sgu_2', 'w_out_2', 'norm_ffn_g_2', 'w_router_group_2',
        'b_router_group_2', 'w_router_expert_2', 'b_router_expert_2', 'w_exp_gate_2', 'w_exp_up_2',
        'w_exp_down_2', 'norm_final_g_2']


def kernel(**inputs):
    import numpy as np
    import concourse.bacc as bacc
    from concourse.bass_utils import run_bass_kernel_spmd

    nc = bacc.Bacc("TRN2", target_bir_lowering=False, num_devices=1)
    arrays, args = {}, []
    for name in _INS:
        a = np.ascontiguousarray(inputs[name])
        arrays[f"in_{name}"] = a
        args.append(nc.dram_tensor(f"in_{name}", a.shape, mybir.dt.from_np(a.dtype), kind="ExternalInput").ap())
    o = nc.dram_tensor("out", inputs["x"].shape, F32, kind="ExternalOutput").ap()
    build_program(nc, *args, o)
    result = run_bass_kernel_spmd(nc, [arrays], core_ids=[0])
    return result.results[0]["out"]
```

```python
from contextlib import ExitStack, contextmanager

import concourse.bass as bass
from concourse import mybir

ALU = mybir.AluOpType
ACT = mybir.ActivationFunctionType
AX_X = mybir.AxisListType.X
F32 = mybir.dt.float32
F32R = mybir.dt.float32r
BF16 = mybir.dt.bfloat16
I32 = mybir.dt.int32

P = 128
PANEL = 2048
RING = 4
BANK = 512
ds = bass.ds


class Tally:

    def __init__(self, sem):
        self.sem, self.base, self.k = sem, 0, 0

    def mark(self, instruction):
        instruction.then_inc(self.sem, 1)
        self.k += 1

    def wait(self, eng, back=0):
        eng.wait_ge(self.sem, self.base + (self.k - back))


@contextmanager
def rounds(eng, count, *counted):
    before = [t.k for t, _ in counted]
    assert all(isinstance(t.base, int) and t.base == 0 for t, _ in counted)
    with eng.Fori(0, count) as i:
        for t, per in counted:
            t.base = i * per
        yield i
    for (t, per), k in zip(counted, before):
        assert t.k == k + per, (t.k - k, per)
        t.base, t.k = 0, k + per * count


def build_program(
    nc, x, meta_tokens, conv_w_in, conv_b_in, conv_w_dw, conv_b_dw, conv_ln_g, conv_ln_b,
    conv_w_out, conv_b_out, norm_mix_pre, norm_mix_post, norm_ffn_pre, norm_ffn_post,
    ffn_w_gate, ffn_w_up, ffn_w_down, norm_mix_g_2, w_in_2, conv_w_2, sgu_ln_g_2, sgu_ln_b_2,
    sgu_w_s_2, sgu_b_s_2, w_up_conv_2, w_up_sgu_2, w_out_2, norm_ffn_g_2, w_router_group_2,
    b_router_group_2, w_router_expert_2, b_router_expert_2, w_exp_gate_2, w_exp_up_2,
    w_exp_down_2, norm_final_g_2, out,
):
    D = x.shape[2]
    T = x.shape[1]
    META = meta_tokens.shape[0]
    TM = META + T
    KT = D // P
    TOK = T // P
    NC = D // BANK
    FF = ffn_w_down.shape[1]
    FT = FF // P
    TAPS = conv_w_dw.shape[1]
    PAD = TAPS - 1 - META
    EXT = PAD + TM
    CW = conv_w_2.shape[2]
    CT = CW // P
    SW = sgu_ln_g_2.shape[1]
    HEADS = sgu_w_s_2.shape[1]
    SBLK = sgu_w_s_2.shape[2]
    HALF = SBLK // 2
    GROUPS = w_router_group_2.shape[2]
    EXPERTS = w_exp_gate_2.shape[1]
    PER = EXPERTS // GROUPS
    DE = w_exp_gate_2.shape[3]
    ET = DE // P
    RMS_EPS, LN_EPS, EPS = 1e-6, 1e-5, 1e-6
    GELU_A = 1.5957691216057308
    GELU_B = GELU_A * 0.044715
    assert T == 2 * P and D == PANEL and SW == HEADS * P and SBLK == P and PAD >= 0 and CW == SW

    A = 0
    B = A + 2 * KT
    C = B + KT
    DN = C + 2 * FT
    ZV = DN + FT
    CH = ZV + 8
    BG = CH + 2 * CT
    U = BG + CT
    GT = U + CT
    UP = GT + 2 * KT
    G = UP + 2 * CT
    MOE = G + KT
    JOB = 3 * PER * ET
    S_B, S_D, S_G = 0, KT, KT + FT
    PE_TAPS, PE_TAPS_LAST = 2, TAPS // 2 - 3
    F_C, F_E = 0, 2 * FT
    F_UP = F_E + (UP - CH)
    F_END = F_UP + 4 * CT

    ctx = ExitStack()
    with ctx:
        arena_at = -(-nc.sbuf_base // 32) * 32

        def sb(name, shape, dt=F32):
            return ctx.enter_context(nc.sbuf_tensor(name, shape, dt))

        def sem(name):
            return ctx.enter_context(nc.semaphore(name))

        BIG = FT * T
        big = sb("big", [P, BIG])
        MR = 2 * KT * P + 2 * D + 2 * P + 2 * P + 2 * 2 * ET * P
        moe_r = nc.alloc_sbuf_tensor_at("moe_r", [P, MR], F32R, offset=arena_at)
        moe_f = nc.alloc_sbuf_tensor_at("moe_f", [P, BIG - MR], F32, offset=arena_at + 4 * MR)
        raw = sb("raw", [P, RING, PANEL])
        whi = sb("whi", [P, 2, PANEL], F32R)
        wlo = sb("wlo", [P, 2, PANEL], F32R)
        xT = sb("xT", [P, KT * 2 * TM], F32R)
        h = sb("h", [P, TOK, D])
        tmp = sb("tmp", [P, TOK, D])
        gB = sb("gB", [P, D])
        act = sb("act", [P, 2, 2, T], F32R)
        vT = sb("vT", [P, 6, P])
        ident = sb("ident", [P, P])
        ones = sb("ones", [P, P])
        wsT = sb("wsT", [P, HEADS, P])
        bsB = sb("bsB", [P, HEADS, P])
        wr = sb("wr", [P, KT, GROUPS + EXPERTS])
        wk = sb("wk", [P, 7 * T])
        st = sb("st", [P, 96])
        sti = sb("sti", [P, 2], I32)
        brow = sb("brow", [1, GROUPS + EXPERTS])
        zrow = sb("zrow", [1, BANK], BF16)
        ps = ctx.enter_context(nc.psum_tensor("ps", [P, 8, BANK], F32))

        xTA = xT[:, :].rearrange("p (k c) -> p k c", k=KT)
        xT5 = xT[:, 0:KT * BANK].rearrange("p (k c) -> p k c", k=KT)
        tH = xT[:, 0:TOK * D].rearrange("p (t d) -> p t d", t=TOK)
        tL = xT[:, TOK * D:2 * TOK * D].rearrange("p (t d) -> p t d", t=TOK)
        uext = big[:, 0:KT * EXT].rearrange("p (k c) -> p k c", k=KT)
        conv_at = KT * EXT + 32
        cv = big[:, conv_at:conv_at + KT * T].rearrange("p (k c) -> p k c", k=KT)
        stage_at = conv_at + KT * T
        vst = big[:, stage_at:stage_at + 6 * P].rearrange("p (r c) -> p r c", r=6)
        wst = big[:, stage_at + 6 * P:stage_at + 6 * P + HEADS * P].rearrange("p (r c) -> p r c", r=HEADS)
        tiles = big[:, :].rearrange("p (k c) -> p k c", c=T)
        UT = 2 * KT
        pext_at = (UT + CT) * T
        pext = big[:, pext_at:pext_at + 2 * (T + 2)].rearrange("p (s c) -> p s c", s=2)
        vbuf = tmp[:, 0, :].rearrange("p (t c) -> p t c", t=TOK)
        vmb = tmp[:, 0, :]
        vscr = tmp[:, 1, :]
        yc = tmp[:, 1, :].rearrange("p (k c) -> p k c", k=CT)
        t1 = wk[:, 0:2 * T].rearrange("p (s c) -> p s c", s=2)
        xs = wk[:, 2 * T:5 * T].rearrange("p (s c) -> p s c", s=3)
        sg = wk[:, 5 * T:7 * T].rearrange("p (s c) -> p s c", s=2)
        sgA = wk[:, 0:2 * TM].rearrange("p (s c) -> p s c", s=2)
        meanb, rstdb = wk[:, 0:T], wk[:, T:2 * T]
        xg = moe_r[:, 0:2 * KT * P].rearrange("p (o k c) -> p o k c", o=2, k=KT)
        yh = moe_r[:, 2 * KT * P:2 * KT * P + 2 * D].rearrange("p (o c) -> p o c", o=2)
        S_at = 2 * KT * P + 2 * D
        Sel = moe_r[:, S_at:S_at + 2 * P].rearrange("p (t c) -> p t c", t=TOK)
        SelT = moe_r[:, S_at + 2 * P:S_at + 4 * P].rearrange("p (t c) -> p t c", t=TOK)
        hT_at = S_at + 4 * P
        hT, hT_last = (moe_r[:, hT_at + b * 2 * ET * P:hT_at + (b + 1) * 2 * ET * P].rearrange("p (o k c) -> p o k c", o=2, k=ET)
                       for b in range(2))
        iota = moe_f[:, 0:P]
        tok_rows = tmp[:, 0, :]
        gsl = tmp[:, 1, 0:DE]
        hid = tmp[:, 1, DE:2 * DE]
        V_PRE, V_BIN, V_BDW, V_LG, V_LB, V_FPRE, V_MIX2 = 0, 16, 48, 64, 80, 96, 112
        V_DW = P
        V_CW2 = 5 * P
        vcol = vT[:, :, :].rearrange("p r c -> p (r c)")
        diag = tmp[:, :, :].rearrange("p t (k c) -> p (t k) c", c=P)

        SSQ, SS, RT, RS, MV, BN, SLOTW = 0, 8, 12, 16, 20, 24, 48
        EPS_AT, LN_EPS_AT, WARM = 88, 89, 90
        OHG = TOK * (GROUPS + EXPERTS) + 2 + 2 * 4 * TOK
        GATE = OHG + 4 * 4 * TOK

        raw_in = [sem(f"raw_in{i}") for i in range(RING)]
        hi_ready = sem("hi_ready")
        lo_pool = sem("lo_pool")
        lo_ready = sem("lo_ready")
        mm_done = sem("mm_done")
        x_in = [sem(f"x_in{t}") for t in range(TOK)]
        meta_in = sem("meta_in")
        vec_in = sem("vec_in")
        ws_in = sem("ws_in")
        bs_in = sem("bs_in")
        wr_in = sem("wr_in")
        gain_in = sem("gain_in")
        ident_ready = sem("ident_ready")
        ones_ready = sem("ones_ready")
        vec_turned = sem("vec_turned")
        vec_ready = sem("vec_ready")
        ws_turned = sem("ws_turned")
        ws_ready = sem("ws_ready")
        ssq_ready = sem("ssq_ready")
        root_ready = sem("root_ready")
        var_ready = sem("var_ready")
        scale_ready = sem("scale_ready")
        xn_ready = sem("xn_ready")
        turned = sem("turned")
        xhi_ready = sem("xhi_ready")
        xlo_ready = sem("xlo_ready")
        pad_ready = sem("pad_ready")
        sig_a = sem("sig_a")
        glu_done = sem("glu_done")
        diag_ready = sem("diag_ready")
        pe_taps = sem("pe_taps")
        conv_done = sem("conv_done")
        sums_done = sem("sums_done")
        cent = sem("cent")
        sq_done = sem("sq_done")
        z_ready = sem("z_ready")
        zs_ready = sem("zs_ready")
        u_ready = sem("u_ready")
        open_done = sem("open_done")
        act_hi = sem("act_hi")
        act_lo = sem("act_lo")
        tok_done = sem("tok_done")
        post_done = sem("post_done")
        feat_half = sem("feat_half")
        feat_free = sem("feat_free")
        sig_c = sem("sig_c")
        hid_ready = sem("hid_ready")
        vsq = sem("vsq")
        varg = sem("varg")
        vsig = sem("vsig")
        v_free = sem("v_free")
        v_norm = sem("v_norm")
        v_ready = sem("v_ready")
        spat_done = sem("spat_done")
        vm_ready = sem("vm_ready")
        usq = sem("usq")
        uarg = sem("uarg")
        usig = sem("usig")
        ut_ready = sem("ut_ready")
        gate_ready = sem("gate_ready")
        ys_ready = sem("ys_ready")
        fused_done = sem("fused_done")
        bias_in = sem("bias_in")
        pair_hi = sem("pair_hi")
        pair_lo = sem("pair_lo")
        thi_ready = sem("thi_ready")
        tlo_ready = sem("tlo_ready")
        tt_turned = sem("tt_turned")
        tt_ready = sem("tt_ready")
        logits_done = sem("logits_done")
        r_shift = sem("r_shift")
        r_exp = sem("r_exp")
        r_mask = sem("r_mask")
        rank_done = sem("rank_done")
        jobs_ready = sem("jobs_ready")
        gates_done = sem("gates_done")
        tri_ready = sem("tri_ready")
        sel_ready = sem("sel_ready")
        slot_done = sem("slot_done")
        selT_ready = sem("selT_ready")
        gath_done = sem("gath_done")
        rows_ready = sem("rows_ready")
        rows_turned = sem("rows_turned")
        xg_hi = sem("xg_hi")
        xg_lo = sem("xg_lo")
        sig_g = sem("sig_g")
        gsl_ready = sem("gsl_ready")
        hid_e = sem("hid_e")
        hid_turned = sem("hid_turned")
        hT_hi = sem("hT_hi")
        hT_lo = sem("hT_lo")
        y_hi = sem("y_hi")
        y_lo = sem("y_lo")
        scat_done = sem("scat_done")
        add_done = sem("add_done")
        fin_ready = sem("fin_ready")
        out_done = sem("out_done")
        act_own = sem("act_own")
        dve_own = sem("dve_own")
        pool_own = sem("pool_own")

        w_exp_g = w_exp_gate_2.rearrange("l e d f -> (l e d) f")
        w_exp_u = w_exp_up_2.rearrange("l e d f -> (l e d) f")
        w_exp_d = w_exp_down_2.rearrange("l e f d -> (l e f) d")

        block = ctx.enter_context(nc.Block())

        @block.sync
        def _(sp):
            def panel(n, s, src, rows, first=False):
                slot = s % RING
                if not first:
                    if isinstance(n, int) and n + s - RING < B:
                        sp.wait_ge(lo_pool, n + s - RING + 1)
                    else:
                        sp.wait_ge(lo_ready, n + (s - RING - B + 1))
                dst = raw[:, slot, :].rearrange("p (k c) -> p k c", c=rows)
                sp.dma_start(dst, src).then_inc(raw_in[slot], 16)

            def columns(w, c, width=P):
                return w[:, ds(c, width)].rearrange("(k p) n -> p k n", p=P)

            def rows_of(w, r):
                return w[ds(r, P), :].rearrange("(a p) n -> p a n", p=P)

            for t in range(TOK):
                sp.dma_start(h[:, t, :], x[0, t * P:(t + 1) * P, :]).then_inc(x_in[t], 16)
            for src, at in ((norm_mix_pre, V_PRE), (conv_b_in, V_BIN), (conv_b_dw, V_BDW), (conv_ln_g, V_LG),
                            (conv_ln_b, V_LB), (norm_ffn_pre, V_FPRE), (norm_mix_g_2, V_MIX2)):
                r = src.rearrange("a (k p) -> (a k) p", p=P)
                sp.dma_start(vst[at:at + r.shape[0], 0, :], r).then_inc(vec_in, 16)
            taps = conv_w_dw[0].rearrange("t (k p) -> (t k) p", p=P)
            for q in range(4):
                r = min(P, TAPS * KT - q * P)
                sp.dma_start(vst[0:r, 1 + q, :], taps[q * P:q * P + r, :]).then_inc(vec_in, 16)
            sp.dma_start(vst[0:3 * CT, 5, :], conv_w_2[0].rearrange("t (k p) -> (t k) p", p=P)).then_inc(vec_in, 16)
            w_in = conv_w_in[0]
            for s in range(4):
                m, g = divmod(s, 2)
                panel(0, s, columns(w_in, g * D + m * P), P, first=True)
            with sp.Fori(1, B // 4) as r:
                n = r * 4
                for s in range(4):
                    m, g = divmod(s, 2)
                    slot = s
                    sp.wait_ge(lo_pool, n + (s - RING + 1))
                    dst = raw[:, slot, :].rearrange("p (k c) -> p k c", c=P)
                    sp.dma_start(dst, columns(w_in, n * (P // 2) + (g * D + m * P))).then_inc(raw_in[slot], 16)
            for s in range(4):
                panel(B, s, rows_of(conv_w_out[0], s * P), D)
            with sp.Fori(1, (KT) // 4) as r:
                j = r * 4
                for s in range(4):
                    panel(j + B, s, rows_of(conv_w_out[0], (j + s) * P), D)
            with sp.Fori(0, (2 * FT) // 4) as r:
                j = r * 4
                for s in range(4):
                    m, g = divmod(s, 2)
                    panel(j + C, s, columns((ffn_w_gate, ffn_w_up)[g][0], j * (P // 2) + m * P), P)
            with sp.Fori(0, (FT) // 4) as r:
                j = r * 4
                for s in range(4):
                    panel(j + DN, s, rows_of(ffn_w_down[0], (j + s) * P), D)
            with sp.Fori(0, (8) // 4) as r:
                j = r * 4
                for s in range(4):
                    src = w_in_2[0, ds((j + s) * (2 * P), 2 * P), 3 * CW + SW:3 * CW + 2 * SW]
                    panel(j + ZV, s, src.rearrange("(k p) n -> p k n", p=P), SW)
            with sp.Fori(0, (2 * CT) // 4) as r:
                j = r * 4
                for s in range(4):
                    m, g = divmod(s, 2)
                    panel(j + CH, s, columns(w_in_2[0], j * (P // 2) + (m * P + (1 + g) * CW)), P)
            for first, col, count in ((BG, 0, CT), (U, 3 * CW, CT), (GT, 3 * CW + 2 * SW, 2 * KT)):
                with sp.Fori(0, (count) // 4) as r:
                    j = r * 4
                    for s in range(4):
                        panel(j + first, s, columns(w_in_2[0], (j + s) * P + col), P)
            with sp.Fori(0, (2 * CT) // 4) as r:
                j = r * 4
                for s in range(4):
                    m, g = divmod(s, 2)
                    w = (w_up_conv_2, w_up_sgu_2)[g][0]
                    panel(j + UP, s, columns(w, j * P + m * 2 * P, 2 * P), 2 * P)
            with sp.Fori(0, (KT) // 4) as r:
                j = r * 4
                for s in range(4):
                    panel(j + G, s, rows_of(w_out_2[0], (j + s) * P), D)

            def expert_in(w, n, s0, e):
                for q in range(4):
                    src = w[ds(e * D + q * (ET * P), ET * P), :].rearrange("(k p) f -> p k f", p=P)
                    panel(n, s0 + q, src, DE)

            def expert_down(n, s0, e):
                for r in range(ET):
                    panel(n, s0 + r, w_exp_d[ds(e * DE + r * P, P), :].rearrange("(a p) n -> p a n", p=P), D)

            def job(n, e0):
                expert_in(w_exp_g, n, 0, e0)
                expert_in(w_exp_u, n, 4, e0)
                with sp.Fori(0, PER - 1) as e:
                    expert_in(w_exp_g, n + e * 12, 8, e0 + e + 1)
                    expert_in(w_exp_u, n + e * 12, 12, e0 + e + 1)
                    expert_down(n + e * 12, 16, e0 + e)
                expert_down(n, JOB - 4, e0 + (PER - 1))

            with sp.Fori(0, GROUPS) as g:
                job(g * JOB + MOE, g * PER)
            sp.wait_ge(jobs_ready, 1)
            extra = nc.sync.value_load(sti[0:1, 0:1], min_val=GROUPS, max_val=GROUPS + 1)
            over = nc.sync.value_load(sti[0:1, 1:2], min_val=0, max_val=GROUPS - 1)
            with sp.If(extra > GROUPS):
                job(MOE + GROUPS * JOB, over * PER)
            sp.end_ifs()
            sp.wait_ge(fin_ready, 2)
            sp.dma_start(out[0].rearrange("(t p) d -> p t d", p=P), tmp[:, :, :]).then_inc(out_done, 16)
            sp.wait_ge(out_done, 16)

        @block.gpsimd
        def _(pool):
            own = Tally(pool_own)
            own.mark(pool.memset(ident[:, :], 0.0))
            pool.memset(ones[:, :], 1.0).then_inc(ones_ready, 1)
            pool.memset(zrow[:, :], 0.0).then_inc(ones_ready, 1)
            own.wait(pool)
            pool.affine_select(out=ident[:, :], in_=ident[:, :], compare_op=ALU.not_equal, fill=1.0, base=0,
                               pattern=[[-1, P]], channel_multiplier=1).then_inc(ident_ready, 1)
            pool.wait_ge(ssq_ready, 3)
            pool.memset(uext[:, :, 0:PAD], 0.0).then_inc(pad_ready, 1)
            with pool.Fori(0, KT // 2) as r:
                n = r * 4
                for s in range(4):
                    pool.wait_ge(hi_ready, n + (s + 1))
                    pool.tensor_tensor(wlo[:, s % 2, :], raw[:, s, :], whi[:, s % 2, :], ALU.subtract).then_inc(lo_pool, 1)

            pool.dma_start(bsB[:, :, :].rearrange("p h i -> p (h i)"),
                           sgu_b_s_2.rearrange("l h i -> l (h i)").to_broadcast([P, HEADS * SBLK])).then_inc(bs_in, 16)
            pool.dma_start(brow[:, 0:GROUPS], b_router_group_2).then_inc(bias_in, 16)
            pool.dma_start(brow[:, GROUPS:GROUPS + EXPERTS], b_router_expert_2).then_inc(bias_in, 16)
            pool.wait_ge(turned, 16)
            pool.dma_start(gB[0:1, :], conv_b_out).then_inc(gain_in, 16)
            pool.wait_ge(open_done, 1)
            pool.dma_start(gB[:, :], norm_mix_post.to_broadcast([P, D])).then_inc(gain_in, 16)
            pool.wait_ge(post_done, 8)
            pool.dma_start(gB[:, :], norm_ffn_post.to_broadcast([P, D])).then_inc(gain_in, 16)
            pool.wait_ge(post_done, 16)
            pool.dma_start(gB[:, 0:SW], sgu_ln_g_2.to_broadcast([P, SW])).then_inc(gain_in, 16)
            pool.dma_start(gB[:, SW:2 * SW], sgu_ln_b_2.to_broadcast([P, SW])).then_inc(gain_in, 16)
            pool.wait_ge(gain_in, 80)
            for t in range(TOK):
                pool.wait_ge(v_norm, t + 1)
                own.mark(pool.tensor_tensor(vbuf[:, t, :], vbuf[:, t, :], gB[:, 0:SW], ALU.mult))
                own.wait(pool)
                pool.tensor_tensor(vbuf[:, t, :], vbuf[:, t, :], gB[:, SW:2 * SW], ALU.add).then_inc(v_ready, 1)
            pool.wait_ge(v_ready, 2)
            pool.dma_start(gB[:, :], norm_ffn_g_2.to_broadcast([P, D])).then_inc(gain_in, 16)
            pool.wait_ge(vm_ready, 4)
            for m in range(CT):
                pool.wait_ge(ut_ready, m + 1 + 2)
                pool.tensor_tensor(tiles[:, UT + m, :], tiles[:, UT + m, :], vmb[:, m * T:(m + 1) * T],
                                   ALU.mult).then_inc(ys_ready, 1)
            pool.wait_ge(xn_ready, 7 + 2)
            pool.dma_start(gB[:, :], norm_final_g_2.rearrange("(a d) -> a d", a=1).to_broadcast([P, D])).then_inc(gain_in, 16)
            pool.wait_ge(spat_done, 1)
            own.mark(pool.memset(wsT[:, 0, :], 1.0))
            own.wait(pool)
            pool.affine_select(out=wsT[:, 0, :], in_=wsT[:, 0, :], compare_op=ALU.is_gt, fill=0.0, base=0,
                               pattern=[[1, P]], channel_multiplier=-1).then_inc(tri_ready, 1)
            pool.wait_ge(mm_done, MOE)
            pool.iota(iota.bitcast(I32), pattern=[[1, P]], base=1, channel_multiplier=0).then_inc(tri_ready, 1)
            pool.memset(SelT.bitcast(F32), 0.0).then_inc(tri_ready, 1)

        @block.scalar
        def _(a):
            own = Tally(act_own)
            fn = nc.scalar.activation

            def hi(n, s):
                if not (isinstance(n, int) and n + s < 2):
                    a.wait_ge(mm_done, n + (s - 1))
                a.wait_ge(raw_in[s % RING], n * 4 + (16 * (s // RING) + 16))
                fn(whi[:, s % 2, :], raw[:, s % RING, :], ACT.Copy).then_inc(hi_ready, 1)

            def root(src, dst, scale, eps):
                fn(dst, src, ACT.Sqrt, bias=eps, scale=scale).then_inc(root_ready, 1)

            def warm(q):
                fn(st[:, WARM + q:WARM + q + 1], st[:, EPS_AT:EPS_AT + 1], ACT.Sqrt)

            def squares(src, t, rows_in=P):
                fn(tiles[0:rows_in, 8 * t:8 * t + 8, :].rearrange("p k c -> p (k c)"), src, ACT.Square,
                   accum_out=st[0:rows_in, SS + t:SS + t + 1]).then_inc(ssq_ready, 1)

            a.dma_start(gB[0:META, :], meta_tokens).then_inc(meta_in, 16)
            a.wait_ge(var_ready, 3)
            warm(2)
            a.wait_ge(x_in[0], 16)
            squares(h[:, 0, :], 0)
            a.wait_ge(meta_in, 16)
            squares(gB[0:META, :], 2, META)
            a.wait_ge(x_in[1], 16)
            squares(h[:, 1, :], 1)
            a.wait_ge(ssq_ready, 3)
            root(st[:, SS:SS + 3], st[:, RT:RT + 3], 1.0 / D, st[:, EPS_AT:EPS_AT + 1])

            a.wait_ge(scale_ready, 1)
            fn(tmp[:, 0, :], h[:, 0, :], ACT.Copy, scale=st[:, RS:RS + 1]).then_inc(xn_ready, 1)
            hi(0, 0)
            a.dma_start(wst, sgu_w_s_2[0].rearrange("h i j -> i h j")).then_inc(ws_in, 16)
            a.dma_start(wr[:, :, 0:GROUPS], w_router_group_2[0].rearrange("(k p) g -> p k g", p=P)).then_inc(wr_in, 16)
            a.dma_start(wr[:, :, GROUPS:GROUPS + EXPERTS],
                        w_router_expert_2[0].rearrange("(k p) g -> p k g", p=P)).then_inc(wr_in, 16)

            a.wait_ge(vec_ready, 1)
            for k in range(KT):
                a.wait_ge(turned, k + 1)
                fn(xTA[:, k, 0:TM], ps[:, k % 4, 0:TM], ACT.Copy,
                   scale=vcol[:, V_PRE + k:V_PRE + k + 1]).then_inc(xhi_ready, 1)
            hi(0, 1)

            def a_group(g):
                for s in range(4):
                    m = s // 2
                    if s % 2:
                        a.wait_ge(glu_done, g * 2 + (m + 2 - 1))
                    hi(g * 4, s + 2)
                    if s % 2:
                        fn(sgA[:, m, :], ps[:, 4 + s, 0:TM], ACT.Sigmoid,
                           bias=vcol[:, ds(g * 2 + (V_BIN + KT + m), 1)]).then_inc(sig_a, 1)

            def diagonals(g, count):
                a.wait_ge(pe_taps, g * 2 + 2)
                for m in range(2):
                    for q in range(count):
                        tap = TAPS - count + q
                        fn(diag[:, m * KT + q, :], ident[:, :], ACT.Copy,
                           scale=vcol[:, ds(g * 2 + (V_DW + tap * KT + m), 1)]).then_inc(diag_ready, 1)

            with a.Fori(0, KT // 2 - 1) as g:
                a_group(g)
                diagonals(g, PE_TAPS)
            a_group(KT // 2 - 1)
            diagonals(KT // 2 - 1, PE_TAPS_LAST)

            warm(3)
            for q in range(4):
                a.wait_ge(cent, q + 1)
                fn(tmp[:, q // 2, (q % 2) * 4 * T:(q % 2 + 1) * 4 * T],
                   cv[:, 4 * q:4 * q + 4, :].rearrange("p k c -> p (k c)"), ACT.Square).then_inc(sq_done, 1)
            a.wait_ge(ws_turned, 1)
            for b in range(2):
                fn(wsT[:, 4 * b:4 * b + 4, :].rearrange("p h i -> p (h i)"), ps[:, 2 + b, :], ACT.Copy).then_inc(ws_ready, 1)
            a.wait_ge(sums_done, 2)
            root(ps[:, 1, 0:T], rstdb, 1.0 / D, st[:, LN_EPS_AT:LN_EPS_AT + 1])

            def silu_tile(j, s):
                a.wait_ge(z_ready, j + (s + 1))
                a.wait_ge(u_ready, j + (s - 1 + 2))
                fn(sg[:, s % 2, :], xs[:, s % 2, :], ACT.Sigmoid).then_inc(zs_ready, 1)

            def split_act(src, step, s, panel, ready=None):
                if ready is not None:
                    a.wait_ge(ready[0], ready[1])
                if panel is not None:
                    a.wait_ge(mm_done, panel - 1)
                fn(act[:, s % 2, 0, :], src, ACT.Copy).then_inc(act_hi, 1)

            def tile_of(v, j, s):
                if isinstance(j, int):
                    return v[:, j + s, :]
                return v[:, ds(j + s, 1), :].rearrange("p a c -> p (a c)")

            for s in range(4):
                if s < 2:
                    silu_tile(0, s)
                if s >= 2:
                    split_act(xs[:, s % 2, :], S_B, s - 2, B + s - 2, (u_ready, s - 1 + 2))
                    silu_tile(0, s)

            def b_group(j, last=False):
                for s in range(4):
                    if not (last and s == 3):
                        hi(j + B, s + 2)
                    if not (last and s >= 2):
                        split_act(xs[:, s % 2, :], S_B, s, None, (u_ready, j + (s + 3 + 2)))
                    if not last:
                        silu_tile(j, s + 4)

            with a.Fori(0, (KT - 4) // 4) as r:
                j = r * 4
                b_group(j)
            b_group(KT - 4, last=True)

            def post(q, n):
                warm(q)
                for t in range(TOK):
                    if t == 0:
                        a.wait_ge(tok_done, q + 1)
                    else:
                        a.wait_ge(mm_done, n)
                    for c in range(NC):
                        b = t * NC + c
                        if b >= 3:
                            a.wait_ge(ssq_ready, 3 + 10 * q + b - 2)
                        fn(wk[:, (b % 3) * BANK:(b % 3 + 1) * BANK], ps[:, b, :], ACT.Square,
                           accum_out=st[:, SSQ + b:SSQ + b + 1]).then_inc(ssq_ready, 1)
                        if b in (NC, TOK * NC - 1):
                            u = b // NC - (b == NC)
                            a.wait_ge(var_ready, 3 + 2 * q + u + 1)
                            root(st[:, SS + u:SS + u + 1], st[:, RT + u:RT + u + 1], 1.0 / D, st[:, EPS_AT:EPS_AT + 1])
                pre(3 + 10 * q + 8, 8 * (q + 1), n)

            def pre(ssq_at, added, n=None):
                for t in range(TOK):
                    if t and n is not None:
                        hi(n, 1)
                    a.wait_ge(add_done, added - 4 * (TOK - 1 - t))
                    fn(tmp[:, t, :], h[:, t, :], ACT.Square, accum_out=st[:, SS + t:SS + t + 1]).then_inc(ssq_ready, 1)
                    a.wait_ge(ssq_ready, ssq_at + t + 1)
                    root(st[:, SS + t:SS + t + 1], st[:, RT + t:RT + t + 1], 1.0 / D, st[:, EPS_AT:EPS_AT + 1])

            def turn(count, gain, bank):
                for k in range(KT):
                    a.wait_ge(turned, KT * count + k + 1 + (k + 1) % 2)
                    b = bank + k // 2 % 4
                    fn(xT5[:, k, 0:T], ps[:, b, k % 2 * T:k % 2 * T + T], ACT.Copy,
                       scale=vcol[:, gain + k:gain + k + 1]).then_inc(xhi_ready, 1)

            post(0, C)
            turn(1, V_FPRE, 0)

            def half(f, s, bank):
                a.wait_ge(feat_free, f + (s + 4 - 1))
                fn(t1[:, s % 2, :], ps[:, bank, T:2 * T], ACT.Copy).then_inc(feat_half, 1)

            with a.Fori(0, FT // 2) as g:
                for s in range(4):
                    a.wait_ge(mm_done, g * 4 + (C + s + 1))
                    half(g * 4 + F_C, s, 4 + s)
                    hi(g * 4 + C, s + 2)
                    if s % 2:
                        a.wait_ge(feat_free, g * 4 + (F_C + s + 4))
                        a.wait_ge(hid_ready, g * 2 + (s // 2 + 2 - 1))
                        fn(sg[:, s // 2, :], xs[:, s // 2, :], ACT.Sigmoid).then_inc(sig_c, 1)

            def rows(n0, src, step, count, ready):
                def group(j, last=False):
                    for s in range(4):
                        if not (last and s == 3):
                            hi(j + n0, s + 2)
                        if not (last and s >= 2):
                            split_act(tile_of(src, j, s + 2), step, s, None)
                for s in range(2):
                    split_act(src[:, s, :], step, s, n0 + s, ready)
                with a.Fori(0, (count - 4) // 4) as r:
                    j = r * 4
                    group(j)
                return group(count - 4, last=True)

            rows(DN, tiles, S_D, FT, (hid_ready, FT + 2))
            post(1, ZV)
            turn(2, V_MIX2, 4)

            for q in range(8):
                hi(ZV, q + 2)
            for b in range(4):
                fn(vscr[:, b * BANK:(b + 1) * BANK], ps[:, b, :], ACT.Square).then_inc(vsq, 1)
            for b in range(4):
                a.wait_ge(varg, b + 1)
                fn(vscr[:, b * BANK:(b + 1) * BANK], vscr[:, b * BANK:(b + 1) * BANK], ACT.Sigmoid).then_inc(vsig, 1)
            hi(CH, 2)
            for t in range(TOK):
                a.wait_ge(var_ready, 7 + t + 1)
                fn(st[:, RT + t:RT + t + 1], st[:, MV + 2 * t + 1:MV + 2 * t + 2], ACT.Sqrt, bias=st[:, EPS_AT:EPS_AT + 1]).then_inc(root_ready, 1)

            def halves(n0, f0, j, first=False):
                for s in range(4):
                    a.wait_ge(mm_done, j + (n0 + s + 1))
                    half(j + f0, s, 4 + s)
                    if not (first and s == 0):
                        hi(j + n0, s + 2)

            halves(CH, F_E, 0, first=True)
            with a.Fori(1, 2 * CT // 4) as r:
                halves(CH, F_E, r * 4)
            with a.Fori(0, CT // 4) as r:
                halves(BG, F_E + BG - CH, r * 4)
            with a.Fori(0, (CT) // 4) as r:
                j = r * 4
                for s in range(4):
                    f = F_E + U - CH
                    a.wait_ge(mm_done, j + (U + s + 1))
                    half(j + f, s, 4 + s)
                    hi(j + U, s + 2)
                    a.wait_ge(feat_free, j + (f + s + 5))
                    fn(sg[:, s % 2, :], xs[:, s % 2, :], ACT.Square).then_inc(usq, 1)
                    a.wait_ge(uarg, j + (s + 1))
                    fn(sg[:, s % 2, :], sg[:, s % 2, :], ACT.Sigmoid).then_inc(usig, 1)
            a.sem_inc(gate_ready, 2)
            def gt_group(j, last=False):
                for s in range(4):
                    f = F_E + GT - CH
                    a.wait_ge(mm_done, j + (GT + s + 1))
                    half(j + f, s, 4 + s)
                    a.wait_ge(feat_free, j + (f + s + 5))
                    if not (last and s == 3):
                        hi(j + GT, s + 2)
                    fn(tile_of(tiles, j, s), xs[:, s % 2, :], ACT.Sigmoid).then_inc(gate_ready, 1)

            with a.Fori(0, (2 * KT - 4) // 4) as r:
                gt_group(r * 4)
            gt_group(2 * KT - 4, last=True)

            a.wait_ge(mm_done, UP)
            for q in range(4):
                src = yc if q < 2 else tiles[:, UT:UT + CT, :]
                k = (q % 2) * 4
                if q == 2:
                    a.wait_ge(ys_ready, CT)
                fn(xT5[:, 4 * q:4 * q + 4, 0:T], src[:, k:k + 4, :], ACT.Copy).then_inc(pair_hi, 1)
                if q == 1:
                    hi(UP, 1)

            with a.Fori(0, (2 * CT) // 4) as r:
                j = r * 4
                for s in range(4):
                    a.wait_ge(mm_done, j + (UP + s + 1))
                    for b in range(2):
                        half(j * 2 + F_UP, 2 * s + b, 4 + (2 * s + b) % 4)
                    hi(j + UP, s + 2)

            for s in range(2):
                a.wait_ge(fused_done, 1)
                fn(act[:, s, 0, :], tiles[:, s, :], ACT.Copy).then_inc(act_hi, 1)

            def g_group(j, last=False):
                for s in range(4):
                    if not (last and s >= 2):
                        hi(j + G, s + 2)
                        split_act(tile_of(tiles, j, s + 2), S_G, s, None)
            with a.Fori(0, (KT - 4) // 4) as r:
                j = r * 4
                g_group(j)
            g_group(KT - 4, last=True)

            warm(4)
            pre(23, 24)
            for t in range(TOK):
                a.wait_ge(xn_ready, 7 + t + 1)
                fn(tH[:, t, :], tmp[:, t, :], ACT.Copy).then_inc(thi_ready, 1)
            for q in range(8):
                a.wait_ge(tt_turned, q + 1)
                fn(tiles[:, 2 * q:2 * q + 2, :].rearrange("p k c -> p (k c)"), ps[:, q, :], ACT.Copy).then_inc(tt_ready, 1)
            a.wait_ge(r_shift, 1)
            fn(st[:, 64:72], st[:, 56:64], ACT.Exp).then_inc(r_exp, 1)
            def gathered(count, q):
                a.wait_ge(gath_done, count + (q + 1))
                fn(tok_rows[:, q * BANK:(q + 1) * BANK], ps[:, 0, :], ACT.Copy).then_inc(rows_ready, 1)

            def gathered_hi(count, q):
                a.wait_ge(rows_turned, count + (q + 1))
                fn(xg[:, 0, 4 * q:4 * q + 4, :].rearrange("p k c -> p (k c)"), ps[:, 3 - 2 * (q % 2), :], ACT.Copy).then_inc(xg_hi, 1)

            def turned_hi(count, dst):
                a.wait_ge(hid_turned, count)
                fn(dst[:, 0, :, :].rearrange("p k c -> p (k c)"), ps[:, 2, :], ACT.Copy).then_inc(hT_hi, 1)

            def result_hi():
                for c in range(NC):
                    fn(yh[:, 0, c * BANK:(c + 1) * BANK], ps[:, 4 + c, :], ACT.Copy).then_inc(y_hi, 1)

            def silu_gate():
                fn(gsl, ps[:, 0, :], ACT.Sigmoid).then_inc(sig_g, 1)

            gathered(0, 0)
            for q in range(4):
                if q < 3:
                    gathered(0, q + 1)
                gathered_hi(0, q)
            a.wait_ge(r_shift, 2)
            fn(st[:, 80:88], st[:, 72:80], ACT.Exp).then_inc(r_exp, 1)
            a.wait_ge(jobs_ready, 1)
            jobs = nc.scalar.value_load(sti[0:1, 0:1], min_val=GROUPS, max_val=GROUPS + 1)
            with a.Fori(0, jobs) as jb:
                n = jb * JOB + MOE
                hi(n, 0)
                hi(n, 1)
                result_hi()
                for q in range(2, 6):
                    hi(n, q)
                silu_gate()
                hi(n, 6)
                hi(n, 7)
                a.wait_ge(slot_done, jb + 1)
                fn(SelT, ps[:, 3, 0:2 * P].rearrange("p (t c) -> p t c", t=TOK), ACT.Copy).then_inc(selT_ready, 1)
                fn(st[:, SLOTW:SLOTW + PER], ps[:, 3, 2 * P:2 * P + PER], ACT.Copy).then_inc(selT_ready, 1)

                def gate_up(n, s0, turn_at):
                    for q in range(6):
                        hi(n, s0 + q)
                    turned_hi(turn_at, hT)
                    silu_gate()
                    hi(n, s0 + 6)
                    hi(n, s0 + 7)

                with a.Fori(0, PER - 2) as e:
                    gate_up(n + e * 12, 8, jb * PER + e + 1)
                    for r in range(4):
                        hi(n + e * 12, 16 + r)
                gate_up(n, JOB - 16, jb * PER + PER - 1)
                hi(n, JOB - 8)
                gathered(jb * 4 + 4, 0)
                hi(n, JOB - 7)
                gathered(jb * 4 + 4, 1)
                hi(n, JOB - 6)
                gathered_hi(jb * 4 + 4, 0)
                gathered(jb * 4 + 4, 2)
                hi(n, JOB - 5)
                turned_hi(jb * PER + PER, hT_last)
                gathered_hi(jb * 4 + 4, 1)
                hi(n, JOB - 4)
                gathered(jb * 4 + 4, 3)
                gathered_hi(jb * 4 + 4, 2)
                hi(n, JOB - 3)
                hi(n, JOB - 2)
                gathered_hi(jb * 4 + 4, 3)
                hi(n, JOB - 1)
            a.wait_ge(mm_done, jobs * JOB + MOE)
            result_hi()
            for t in range(TOK):
                a.wait_ge(add_done, jobs * 8 + (24 + NC * (t + 1)))
                fn(tmp[:, t, :], h[:, t, :], ACT.Square, accum_out=st[:, SS + t:SS + t + 1]).then_inc(ssq_ready, 1)
                a.wait_ge(ssq_ready, 25 + t + 1)
                root(st[:, SS + t:SS + t + 1], st[:, RT + t:RT + t + 1], 1.0 / D, st[:, EPS_AT:EPS_AT + 1])

        @block.vector
        def _(v):
            own = Tally(dve_own)
            V = nc.vector

            def lo(n, s):
                v.wait_ge(hi_ready, n + (s + 1))
                V.tensor_tensor(wlo[:, s % 2, :], raw[:, s % RING, :], whi[:, s % 2, :], ALU.subtract).then_inc(lo_ready, 1)

            def flat(x3):
                return x3.rearrange("p k c -> p (k c)")

            def tile_of(t, j, s):
                if isinstance(j, int):
                    return t[:, j + s, :]
                return t[:, ds(j + s, 1), :].rearrange("p a c -> p (a c)")

            V.memset(st[:, 0:EPS_AT], 0.0).then_inc(var_ready, 1)
            V.memset(st[:, EPS_AT:EPS_AT + 1], RMS_EPS).then_inc(var_ready, 1)
            V.memset(st[:, LN_EPS_AT:LN_EPS_AT + 1], LN_EPS).then_inc(var_ready, 1)
            v.wait_ge(vec_turned, 1)
            V.tensor_copy(flat(vT[:, 0:4, :]), ps[:, 0, :])
            V.tensor_copy(vT[:, 4, 0:TAPS * KT - 3 * P], ps[:, 1, 0:TAPS * KT - 3 * P])
            V.tensor_copy(vT[:, 5, 0:3 * CT], ps[:, 1, P:P + 3 * CT]).then_inc(vec_ready, 1)
            v.wait_ge(root_ready, 1)
            V.reciprocal(st[:, RS:RS + 3], st[:, RT:RT + 3]).then_inc(scale_ready, 1)
            v.wait_ge(scale_ready, 1)
            V.tensor_scalar(tmp[:, 1, :], h[:, 1, :], st[:, RS + 1:RS + 2], None, ALU.mult).then_inc(xn_ready, 1)
            V.tensor_scalar(gB[0:META, :], gB[0:META, :], st[0:META, RS + 2:RS + 3], None, ALU.mult).then_inc(xn_ready, 1)
            for k in range(KT):
                v.wait_ge(xhi_ready, k + 1)
                V.scalar_tensor_tensor(out=xTA[:, k, TM:2 * TM], in0=ps[:, k % 4, 0:TM],
                                       scalar=vcol[:, V_PRE + k:V_PRE + k + 1], in1=xTA[:, k, 0:TM],
                                       op0=ALU.mult, op1=ALU.subtract).then_inc(xlo_ready, 1)
            v.sem_inc(glu_done, 2)
            v.wait_ge(pad_ready, 1)

            def glu(g, m):
                v.wait_ge(sig_a, g * 2 + (m + 1))
                V.scalar_tensor_tensor(out=uext[:, ds(g * 2 + m, 1), PAD:EXT].rearrange("p a c -> p (a c)"),
                                       in0=ps[:, 4 + 2 * m, 0:TM], scalar=vcol[:, ds(g * 2 + (V_BIN + m), 1)],
                                       in1=sgA[:, m, :], op0=ALU.add, op1=ALU.mult).then_inc(glu_done, 1)

            def conv_pair(g, taken, last=False):
                dsts = [cv[:, ds(g * 2 + m, 1), :].rearrange("p a c -> p (a c)") for m in range(2)]
                for tap in range(TAPS - taken):
                    if tap == TAPS // 2 and not last:
                        glu(g + 1, 0)
                    for m in range(2):
                        src = uext[:, ds(g * 2 + m, 1), tap:tap + T].rearrange("p a c -> p (a c)")
                        w = vcol[:, ds(g * 2 + (V_DW + tap * KT + m), 1)]
                        if tap == 0:
                            v.wait_ge(glu_done, g * 2 + (m + 1 + 2))
                            ins = V.tensor_scalar(dsts[m], src, w, vcol[:, ds(g * 2 + (V_BDW + m), 1)], ALU.mult, ALU.add)
                        else:
                            own.wait(v, 1)
                            ins = V.scalar_tensor_tensor(out=dsts[m], in0=src, scalar=w, in1=dsts[m], op0=ALU.mult, op1=ALU.add)
                        own.mark(ins)
                own.wait(v)
                for m in range(2):
                    v.wait_ge(pe_taps, g * 2 + (m + 1 + 2))
                    V.tensor_tensor(dsts[m], dsts[m], ps[:, 2 + m, 0:T], ALU.add).then_inc(conv_done, 1)
                if not last:
                    glu(g + 1, 1)

            glu(0, 0)
            glu(0, 1)
            with rounds(v, KT // 2 - 1, (own, 2 * (TAPS - PE_TAPS))) as g:
                conv_pair(g, PE_TAPS)
            conv_pair(KT // 2 - 1, PE_TAPS_LAST, last=True)
            v.wait_ge(sums_done, 1)
            own.mark(V.tensor_scalar(meanb, ps[:, 0, 0:T], 1.0 / D, None, ALU.mult))
            own.wait(v)
            for q in range(4):
                V.tensor_tensor(cv[:, 4 * q:4 * q + 4, :], cv[:, 4 * q:4 * q + 4, :],
                                meanb.rearrange("p (a c) -> p a c", a=1).to_broadcast([P, 4, T]), ALU.subtract).then_inc(cent, 1)
            lo(B, 0)
            lo(B, 1)
            v.wait_ge(root_ready, 2)
            own.mark(V.reciprocal(rstdb, rstdb))
            own.wait(v)
            v.sem_inc(u_ready, 2)

            def norm_tile(j, s):
                t = xs[:, s % 2, :]
                if not (isinstance(j, int) and j + s < 2):
                    v.wait_ge(act_lo, j + (s - 1))
                own.mark(V.tensor_tensor(t, tile_of(cv, j, s), rstdb, ALU.mult))
                own.wait(v)
                gcol = vcol[:, ds(j + (V_LG + s), 1)]
                bcol = vcol[:, ds(j + (V_LB + s), 1)]
                V.tensor_scalar(t, t, gcol, bcol, ALU.mult, ALU.add).then_inc(z_ready, 1)

            def silu_tile(j, s):
                v.wait_ge(zs_ready, j + (s + 1))
                t = xs[:, s % 2, :]
                V.tensor_tensor(t, t, sg[:, s % 2, :], ALU.mult).then_inc(u_ready, 1)

            def split_act(src, s, count):
                v.wait_ge(act_hi, count)
                V.tensor_tensor(act[:, s % 2, 1, :], src, act[:, s % 2, 0, :], ALU.subtract).then_inc(act_lo, 1)

            for s in range(4):
                if s >= 2:
                    split_act(xs[:, s % 2, :], s, S_B + s - 1)
                norm_tile(0, s)
                silu_tile(0, s)

            def b_group(j, last=False):
                for s in range(4):
                    if not (last and s >= 2):
                        split_act(xs[:, s % 2, :], s, j + (S_B + s + 3))
                    if not last:
                        norm_tile(j, s + 4)
                    if not (last and s == 3):
                        lo(j + B, s + 2)
                    if not last:
                        silu_tile(j, s + 4)

            v.wait_ge(ws_ready, 2)
            V.memset(wsT[HALF:P, :, 0:HALF], 0.0).then_inc(ws_ready, 1)
            with rounds(v, (KT - 4) // 4, (own, 4)) as r:
                b_group(r * 4)
            b_group(KT - 4, last=True)

            def post(q, gain, n):
                v.wait_ge(gain_in, gain)
                for t in range(TOK):
                    if t:
                        total(q, t)
                    for c in range(NC):
                        v.wait_ge(ssq_ready, 3 + 10 * q + NC * t + c + 1)
                        if c == NC - 1 and t == 0:
                            total(q, t)
                        V.tensor_tensor(tmp[:, t, c * BANK:(c + 1) * BANK], ps[:, t * NC + c, :],
                                        gB[:, c * BANK:(c + 1) * BANK], ALU.mult).then_inc(post_done, 1)
                    v.wait_ge(root_ready, 2 + 4 * q + t + 1)
                    own.mark(V.reciprocal(st[:, RS + t:RS + t + 1], st[:, RT + t:RT + t + 1]))
                    own.wait(v)
                    v.wait_ge(post_done, 8 * q + NC * (t + 1))
                    V.scalar_tensor_tensor(out=h[:, t, :], in0=tmp[:, t, :], scalar=st[:, RS + t:RS + t + 1],
                                           in1=h[:, t, :], op0=ALU.mult, op1=ALU.add).then_inc(add_done, 4)
                pre(3 + 10 * q + 8, 2 + 4 * q + 2)
                lo(n, 1)

            def total(q, t):
                v.wait_ge(ssq_ready, 3 + 10 * q + NC * (t + 1))
                V.reduce_sum(st[:, SS + t:SS + t + 1], st[:, SSQ + NC * t:SSQ + NC * (t + 1)], AX_X).then_inc(var_ready, 1)

            def pre(ssq_at, root_at, gain=None):
                for t in range(TOK):
                    v.wait_ge(ssq_ready, ssq_at + t + 1)
                    v.wait_ge(root_ready, root_at + t + 1)
                    own.mark(V.reciprocal(st[:, RS + t:RS + t + 1], st[:, RT + t:RT + t + 1]))
                    own.wait(v)
                    if gain is None:
                        V.tensor_scalar(tmp[:, t, :], h[:, t, :], st[:, RS + t:RS + t + 1], None, ALU.mult).then_inc(xn_ready, 1)
                    else:
                        v.wait_ge(gain_in, gain)
                        V.scalar_tensor_tensor(out=tmp[:, t, :], in0=h[:, t, :], scalar=st[:, RS + t:RS + t + 1],
                                               in1=gB[:, :], op0=ALU.mult, op1=ALU.mult).then_inc(xn_ready, 1)

            def turn(count, gain, bank):
                for k in range(KT):
                    v.wait_ge(xhi_ready, KT * count + k + 1 + (k + 1) % 2)
                    b = bank + k // 2 % 4
                    V.scalar_tensor_tensor(out=xT5[:, k, T:2 * T], in0=ps[:, b, k % 2 * T:k % 2 * T + T],
                                           scalar=vcol[:, gain + k:gain + k + 1], in1=xT5[:, k, 0:T],
                                           op0=ALU.mult, op1=ALU.subtract).then_inc(xlo_ready, 1)

            post(0, 32, C)
            v.sem_inc(feat_free, 4)
            v.sem_inc(hid_ready, 2)
            turn(1, V_FPRE, 0)

            def joined(f, s, bank, dst):
                v.wait_ge(feat_half, f + (s + 1))
                V.tensor_tensor(dst, ps[:, bank, 0:T], t1[:, s % 2, :], ALU.add).then_inc(feat_free, 1)

            with rounds(v, FT // 2, (own, 2)) as g:
                for s in range(4):
                    if s % 2:
                        v.wait_ge(hid_ready, g * 2 + (s // 2 + 2))
                    joined(g * 4 + F_C, s, 4 + s, xs[:, 2 if s % 2 else s // 2, :])
                    lo(g * 4 + C, s + 2)
                    if s % 2:
                        v.wait_ge(sig_c, g * 2 + (s // 2 + 1))
                        own.mark(V.tensor_tensor(sg[:, s // 2, :], sg[:, s // 2, :], xs[:, s // 2, :], ALU.mult))
                        own.wait(v)
                        v.wait_ge(feat_free, g * 4 + (F_C + s + 5))
                        V.tensor_tensor(tile_of(tiles, g * 2, s // 2), sg[:, s // 2, :], xs[:, 2, :], ALU.mult).then_inc(hid_ready, 1)

            def rows(n0, src, step, count):
                def group(j, last=False):
                    for s in range(4):
                        if not (last and s >= 2):
                            split_act(tile_of(src, j, s + 2), s, j + (step + s + 3))
                        if not (last and s == 3):
                            lo(j + n0, s + 2)
                for s in range(2):
                    split_act(src[:, s, :], s, step + s + 1)
                with v.Fori(0, (count - 4) // 4) as r:
                    j = r * 4
                    group(j)
                group(count - 4, last=True)

            rows(DN, tiles, S_D, FT)
            post(1, 48, ZV)
            turn(2, V_MIX2, 4)

            for q in range(8):
                lo(ZV, q + 2)
            for b in range(4):
                v.wait_ge(vsq, b + 1)
                t = vscr[:, b * BANK:(b + 1) * BANK]
                own.mark(V.tensor_scalar(t, t, GELU_B, GELU_A, ALU.mult, ALU.add))
                own.wait(v)
                V.tensor_tensor(t, t, ps[:, b, :], ALU.mult).then_inc(varg, 1)
            for b in range(4):
                v.wait_ge(vsig, b + 1)
                V.tensor_tensor(vbuf[:, b // 2, (b % 2) * BANK:(b % 2 + 1) * BANK],
                                vscr[:, b * BANK:(b + 1) * BANK], ps[:, b, :], ALU.mult).then_inc(v_free, 1)
            for t in range(TOK):
                v.wait_ge(v_free, 2 * t + 2)
                for c in range(2):
                    own.mark(V.bn_stats(st[:, BN + 12 * t + 6 * c:BN + 12 * t + 6 * c + 6], vbuf[:, t, c * BANK:(c + 1) * BANK]))
                own.wait(v)
                V.bn_aggr(st[:, MV + 2 * t:MV + 2 * t + 2], st[:, BN + 12 * t:BN + 12 * t + 12].rearrange("p (a c) -> p a c", a=2)).then_inc(var_ready, 1)
                if t == 0:
                    lo(CH, 2)
                v.wait_ge(root_ready, 10 + t + 1)
                own.mark(V.reciprocal(st[:, RS + t:RS + t + 1], st[:, RT + t:RT + t + 1]))
                own.wait(v)
                V.tensor_scalar(vbuf[:, t, :], vbuf[:, t, :], st[:, MV + 2 * t:MV + 2 * t + 1],
                                st[:, RS + t:RS + t + 1], ALU.subtract, ALU.mult).then_inc(v_norm, 1)

            own.mark(V.memset(pext[:, :, 0:2], 0.0))
            own.wait(v)
            def ch_group(g, first=False):
                for s in range(4):
                    m = s // 2
                    joined(g * 4 + F_E, s, 4 + s, xs[:, 2 if s % 2 else m, :])
                    if not (first and s == 0):
                        lo(g * 4 + CH, s + 2)
                    if s % 2:
                        v.wait_ge(feat_free, g * 4 + (F_E + s + 5))
                        own.mark(V.tensor_tensor(pext[:, m, 2:T + 2], xs[:, m, :], xs[:, 2, :], ALU.mult))
                        own.wait(v)
                        y = tile_of(yc, g * 2, m)

                        def w(tap):
                            return vcol[:, ds(g * 2 + (V_CW2 + tap * CT + m), 1)]
                        own.mark(V.tensor_scalar(y, pext[:, m, 0:T], w(0), None, ALU.mult))
                        for tap in (1, 2):
                            own.wait(v)
                            own.mark(V.scalar_tensor_tensor(out=y, in0=pext[:, m, tap:tap + T], scalar=w(tap), in1=y,
                                                            op0=ALU.mult, op1=ALU.add))

            ch_group(0, first=True)
            with rounds(v, CT // 2 - 1, (own, 8)) as g:
                ch_group(g + 1)
            own.wait(v)
            with rounds(v, CT // 4, (own, 4)) as r:
                for s in range(4):
                    f = F_E + BG - CH
                    own.wait(v, 1)
                    joined(r * 4 + f, s, 4 + s, xs[:, s % 2, :])
                    lo(r * 4 + BG, s + 2)
                    v.wait_ge(feat_free, r * 4 + (f + s + 5))
                    y = tile_of(yc, r * 4, s)
                    own.mark(V.tensor_tensor(y, y, xs[:, s % 2, :], ALU.mult))
            v.wait_ge(spat_done, 1)
            v.wait_ge(bs_in, 16)
            for b in range(4):
                V.tensor_tensor(vmb[:, b * BANK:(b + 1) * BANK].rearrange("p (h n i) -> p h n i", h=2, n=TOK),
                                ps[:, b, :].rearrange("p (h n i) -> p h n i", h=2, n=TOK),
                                bsB[:, 2 * b:2 * b + 2, :].rearrange("p h (a i) -> p h a i", a=1).to_broadcast([P, 2, TOK, P]),
                                ALU.add).then_inc(vm_ready, 1)
            v.sem_inc(ut_ready, 2)
            own.wait(v)
            with rounds(v, CT // 4, (own, 4)) as r:
                for s in range(4):
                    f = F_E + U - CH
                    v.wait_ge(ut_ready, r * 4 + (s - 1 + 2))
                    joined(r * 4 + f, s, 4 + s, xs[:, s % 2, :])
                    lo(r * 4 + U, s + 2)
                    v.wait_ge(usq, r * 4 + (s + 1))
                    t = sg[:, s % 2, :]
                    own.mark(V.tensor_scalar(t, t, GELU_B, GELU_A, ALU.mult, ALU.add))
                    own.wait(v)
                    V.tensor_tensor(t, t, xs[:, s % 2, :], ALU.mult).then_inc(uarg, 1)
                    v.wait_ge(usig, r * 4 + (s + 1))
                    V.tensor_tensor(tile_of(tiles, r * 4 + UT, s), t, xs[:, s % 2, :], ALU.mult).then_inc(ut_ready, 1)
            v.wait_ge(ut_ready, CT + 2)
            def gt_group(j, last=False):
                for s in range(4):
                    f = F_E + GT - CH
                    v.wait_ge(gate_ready, j + (s - 1 + 2))
                    joined(j + f, s, 4 + s, xs[:, s % 2, :])
                    if not (last and s == 3):
                        lo(j + GT, s + 2)

            with v.Fori(0, (2 * KT - 4) // 4) as r:
                gt_group(r * 4)
            gt_group(2 * KT - 4, last=True)

            own.wait(v)
            for q in range(4):
                src = yc if q < 2 else tiles[:, UT:UT + CT, :]
                k = (q % 2) * 4
                v.wait_ge(pair_hi, q + 1)
                V.tensor_tensor(xT5[:, 4 * q:4 * q + 4, T:2 * T], src[:, k:k + 4, :], xT5[:, 4 * q:4 * q + 4, 0:T],
                                ALU.subtract).then_inc(pair_lo, 1)
                if q == 1:
                    lo(UP, 1)

            v.wait_ge(gate_ready, 2 * KT + 2)
            with rounds(v, CT // 2, (own, 16 - 4)) as r:
                for s in range(4):
                    for b in range(2):
                        i = 2 * s + b
                        m, br = 2 * (s // 2) + b, s % 2
                        own.wait(v)
                        joined(r * 8 + F_UP, i, 4 + i % 4, xs[:, b, :])
                        v.wait_ge(feat_free, r * 8 + (F_UP + i + 5))
                        gate = tile_of(tiles, r * 4 + br * KT, m)
                        own.mark(V.tensor_tensor(gate, gate, xs[:, b, :], ALU.mult))
                        if br:
                            own.wait(v)
                            own.mark(V.tensor_tensor(tile_of(tiles, r * 4, m), tile_of(tiles, r * 4, m), gate, ALU.add))
                    lo(r * 4 + UP, s + 2)
            own.wait(v)
            v.sem_inc(fused_done, 1)

            def g_rows():
                def group(j, last=False):
                    for s in range(4):
                        if not (last and s >= 2):
                            split_act(tile_of(tiles, j, s + 2), s, j + (S_G + s + 3))
                            lo(j + G, s + 2)
                for s in range(2):
                    split_act(tiles[:, s, :], s, S_G + s + 1)
                with v.Fori(0, (KT - 4) // 4) as r:
                    j = r * 4
                    group(j)
                group(KT - 4, last=True)
            g_rows()

            for t in range(TOK):
                if t == 0:
                    v.wait_ge(tok_done, 3)
                else:
                    v.wait_ge(mm_done, MOE)
                for c in range(NC):
                    hc = h[:, t, c * BANK:(c + 1) * BANK]
                    V.tensor_tensor(hc, hc, ps[:, t * NC + c, :], ALU.add).then_inc(add_done, 1)
            pre(23, 12, gain=96)
            for t in range(TOK):
                v.wait_ge(thi_ready, t + 1)
                V.tensor_tensor(tL[:, t, :], tmp[:, t, :], tH[:, t, :], ALU.subtract).then_inc(tlo_ready, 1)

            R = wk[:, 0:512]
            at = [0]

            def cols(n, shape=None):
                r = R[:, at[0]:at[0] + n]
                at[0] += n
                return r

            def step(ins):
                own.mark(ins)
                own.wait(v)

            NL = GROUPS + EXPERTS
            lg = cols(TOK * NL).rearrange("p (t c) -> p t c", t=TOK)
            mx = cols(2)
            pri = cols(8).rearrange("p (t c) -> p t c", t=TOK)
            eq = cols(8).rearrange("p (t c) -> p t c", t=TOK)
            ohg = cols(8).rearrange("p (t c) -> p t c", t=TOK)
            oh1 = cols(8).rearrange("p (t c) -> p t c", t=TOK)
            oh2 = cols(8).rearrange("p (t c) -> p t c", t=TOK)
            sel = cols(8).rearrange("p (t c) -> p t c", t=TOK)
            gate = cols(8).rearrange("p (t c) -> p t c", t=TOK)
            pg = cols(2)
            zz = cols(2)
            rank = cols(2)
            inlow = cols(2)
            slot = cols(TOK * (GROUPS + 2)).rearrange("p (t c) -> p t c", t=TOK)
            ovf = cols(4)
            num = cols(4)
            jf = cols(2)
            assert at[0] <= 512 and OHG == TOK * NL + 2 + 16 and GATE == OHG + 32
            dg = st[:, 56:64].rearrange("p (t c) -> p t c", t=TOK)
            eg = st[:, 64:72].rearrange("p (t c) -> p t c", t=TOK)
            d1 = st[:, 72:80].rearrange("p (t c) -> p t c", t=TOK)
            e1 = st[:, 80:88].rearrange("p (t c) -> p t c", t=TOK)

            def bc(x2, n):
                return x2.rearrange("p (t a) -> p t a", a=1).to_broadcast([P, TOK, n])

            for i in range(GROUPS):
                V.memset(pri[:, :, i], float(GROUPS - i))
                V.memset(num[:, i:i + 1], float(i))
            V.memset(slot[:, :, GROUPS + 1], 0.0)

            def first_max(oh, d):
                step(V.tensor_scalar(eq, d, 0.0, None, ALU.is_equal))
                step(V.tensor_tensor(eq, eq, pri, ALU.mult))
                step(V.reduce_max(mx, eq, AX_X))
                step(V.tensor_tensor(oh, eq, bc(mx, 4), ALU.is_equal))

            def select(jb):
                for t in range(TOK):
                    V.tensor_scalar(Sel[:, t, :], iota, slot[:, t, ds(jb, 1)], None, ALU.is_equal).then_inc(sel_ready, 1)

            v.wait_ge(tri_ready, 2)
            step(V.tensor_copy(iota, iota.bitcast(I32)))
            v.wait_ge(logits_done, 1)
            step(V.tensor_copy(lg, ps[:, 0, 0:2 * 32].rearrange("p (t c) -> p t c", t=2)[:, :, 0:NL]))
            step(V.reduce_max(mx, lg[:, :, 0:GROUPS], AX_X))
            V.tensor_tensor(dg, lg[:, :, 0:GROUPS], bc(mx, 4), ALU.subtract).then_inc(r_shift, 1)
            v.wait_ge(r_shift, 1)
            first_max(ohg, dg)
            v.sem_inc(r_mask, 1)
            v.wait_ge(rank_done, 1)
            rk = ps[:, 1, 0:8].rearrange("p (t c) -> p t c", t=TOK)
            step(V.tensor_tensor(eq, ohg, rk, ALU.mult))
            step(V.reduce_sum(rank, eq, AX_X))
            V.tensor_scalar(ovf, ps[:, 1, 8:12], float(P), None, ALU.is_gt)
            step(V.tensor_scalar(inlow, rank, float(P), None, ALU.is_lt))
            step(V.tensor_scalar(rank, rank, 1.0, None, ALU.add))
            step(V.tensor_tensor(mx, inlow, rank, ALU.mult))
            step(V.tensor_tensor(slot[:, :, 0:GROUPS], ohg, bc(mx, GROUPS), ALU.mult))
            select(0)
            step(V.tensor_tensor(mx, rank, mx, ALU.subtract))
            step(V.tensor_scalar(zz, inlow, float(P), float(-P), ALU.mult, ALU.add))
            step(V.tensor_tensor(slot[:, :, GROUPS], mx, zz, ALU.add))
            step(V.reduce_sum(jf[:, 0:1], ovf, AX_X))
            step(V.tensor_scalar(jf[:, 0:1], jf[:, 0:1], float(GROUPS), None, ALU.add))
            step(V.tensor_tensor(ovf, ovf, num, ALU.mult))
            step(V.reduce_sum(jf[:, 1:2], ovf, AX_X))
            V.tensor_copy(sti[:, :], jf).then_inc(jobs_ready, 1)

            def chosen_logits():
                for t in range(TOK):
                    step(V.tensor_scalar(sel[:, t, :], lg[:, t, GROUPS:GROUPS + PER], ohg[:, t, 0:1], None, ALU.mult))
                    for g in range(1, GROUPS):
                        step(V.scalar_tensor_tensor(out=sel[:, t, :], in0=lg[:, t, GROUPS + PER * g:GROUPS + PER * (g + 1)],
                                                    scalar=ohg[:, t, g:g + 1], in1=sel[:, t, :], op0=ALU.mult, op1=ALU.add))
                step(V.reduce_max(mx, sel, AX_X))
                V.tensor_tensor(d1, sel, bc(mx, 4), ALU.subtract).then_inc(r_shift, 1)
                v.wait_ge(r_shift, 2)

            def chosen_experts():
                first_max(oh1, d1)
                step(V.scalar_tensor_tensor(out=sel, in0=oh1, scalar=-1e30, in1=d1, op0=ALU.mult, op1=ALU.add))
                step(V.reduce_max(mx, sel, AX_X))
                step(V.tensor_tensor(sel, sel, bc(mx, 4), ALU.subtract))
                first_max(oh2, sel)
                step(V.tensor_tensor(oh1, oh1, oh2, ALU.add))

            def chosen_gates():
                v.wait_ge(r_exp, 2)
                step(V.tensor_tensor(gate, oh1, e1, ALU.mult))
                step(V.reduce_sum(zz, gate, AX_X))
                step(V.reduce_sum(pg, eg, AX_X))
                step(V.tensor_tensor(zz, zz, pg, ALU.mult))
                step(V.reciprocal(zz, zz))
                V.tensor_tensor(gate, gate, bc(zz, 4), ALU.mult).then_inc(gates_done, 1)

            def gathered_lo(count, q):
                v.wait_ge(xg_hi, count + (q + 1))
                V.tensor_tensor(flat(xg[:, 1, 4 * q:4 * q + 4, :]), ps[:, 3 - 2 * (q % 2), :], flat(xg[:, 0, 4 * q:4 * q + 4, :]),
                                ALU.subtract).then_inc(xg_lo, 1)

            def turned_lo(count, dst):
                v.wait_ge(hT_hi, count)
                V.tensor_tensor(flat(dst[:, 1, :, :]), ps[:, 2, :], flat(dst[:, 0, :, :]), ALU.subtract).then_inc(hT_lo, 1)

            def result_lo(count, chunks=range(NC)):
                for c in chunks:
                    v.wait_ge(y_hi, count + (c + 1))
                    V.tensor_tensor(yh[:, 1, c * BANK:(c + 1) * BANK], ps[:, 4 + c, :], yh[:, 0, c * BANK:(c + 1) * BANK],
                                    ALU.subtract).then_inc(y_lo, 1)

            def take(t, count, chunks=range(NC), bank=4):
                for c in chunks:
                    v.wait_ge(scat_done, count + (NC * t + c + 1))
                    hc = h[:, t, c * BANK:(c + 1) * BANK]
                    V.tensor_tensor(hc, hc, ps[:, bank + c, :], ALU.add).then_inc(add_done, 1)

            def silu_gate(count):
                v.wait_ge(sig_g, count)
                V.tensor_tensor(gsl, gsl, ps[:, 0, :], ALU.mult).then_inc(gsl_ready, 1)

            def hidden(n, last, weight, count):
                v.wait_ge(mm_done, n + last)
                v.wait_ge(gsl_ready, count)
                V.scalar_tensor_tensor(out=hid, in0=ps[:, 1, :], scalar=st[:, ds(weight, 1)],
                                       in1=gsl, op0=ALU.mult, op1=ALU.mult).then_inc(hid_e, 1)

            gathered_lo(0, 0)
            chosen_logits()
            gathered_lo(0, 1)
            gathered_lo(0, 2)
            gathered_lo(0, 3)
            chosen_experts()
            chosen_gates()
            v.wait_ge(jobs_ready, 1)
            jobs = nc.vector.value_load(sti[0:1, 0:1], min_val=GROUPS, max_val=GROUPS + 1)
            with v.Fori(0, jobs) as jb:
                n = jb * JOB + MOE
                lo(n, 0)
                result_lo(jb * 4, (0, 1))
                lo(n, 1)
                result_lo(jb * 4, (2, 3))
                lo(n, 2)
                take(0, jb * 8, (0,))
                lo(n, 3)
                take(0, jb * 8, (1, 2))
                lo(n, 4)
                take(0, jb * 8, (3,))
                lo(n, 5)
                silu_gate(jb * PER + 1)
                take(1, jb * 8, (0,))
                lo(n, 6)
                take(1, jb * 8, (1, 2))
                lo(n, 7)
                take(1, jb * 8, (3,))
                lo(n, 8)
                v.wait_ge(selT_ready, jb * 2 + 2)
                hidden(n, 8, SLOTW, jb * PER + 1)
                select(jb + 1)

                def gate_up(n, s0, count, turn_at):
                    for q in range(1, 6):
                        lo(n, s0 + q)
                    turned_lo(turn_at, hT)
                    silu_gate(count)
                    lo(n, s0 + 6)
                    lo(n, s0 + 7)

                with v.Fori(0, PER - 2) as e:
                    gate_up(n + e * 12, 8, jb * PER + e + 2, jb * PER + e + 1)
                    lo(n + e * 12, 16)
                    lo(n + e * 12, 17)
                    hidden(n + e * 12, 16, e + (SLOTW + 1), jb * PER + e + 2)
                    lo(n + e * 12, 18)
                    lo(n + e * 12, 19)
                    lo(n + e * 12, 20)
                gate_up(n, JOB - 16, jb * PER + PER, jb * PER + PER - 1)
                lo(n, JOB - 8)
                hidden(n, JOB - 8, SLOTW + PER - 1, jb * PER + PER)
                lo(n, JOB - 7)
                lo(n, JOB - 6)
                gathered_lo(jb * 4 + 4, 0)
                lo(n, JOB - 5)
                turned_lo(jb * PER + PER, hT_last)
                gathered_lo(jb * 4 + 4, 1)
                lo(n, JOB - 4)
                gathered_lo(jb * 4 + 4, 2)
                lo(n, JOB - 3)
                lo(n, JOB - 2)
                gathered_lo(jb * 4 + 4, 3)
                lo(n, JOB - 1)
            result_lo(jobs * 4)
            take(0, jobs * 8)
            take(1, jobs * 8, bank=0)
            for t in range(TOK):
                v.wait_ge(root_ready, 14 + t + 1)
                own.mark(V.reciprocal(st[:, RS + t:RS + t + 1], st[:, RT + t:RT + t + 1]))
                own.wait(v)
                v.wait_ge(gain_in, 112)
                V.scalar_tensor_tensor(out=tmp[:, t, :], in0=h[:, t, :], scalar=st[:, RS + t:RS + t + 1],
                                       in1=gB[:, :], op0=ALU.mult, op1=ALU.mult).then_inc(fin_ready, 1)

        @block.tensor
        def _(pe):
            mm = nc.tensor.matmul
            tr = nc.tensor.transpose

            pe.wait_ge(ident_ready, 1)
            pe.wait_ge(ones_ready, 2)
            pe.wait_ge(vec_in, 16 * 12)
            for r in range(6):
                rows_in = P if r < 4 else (TAPS * KT - 3 * P if r == 4 else 3 * CT)
                t = tr(ps[:, r // 4, (r % 4) * P:(r % 4) * P + rows_in], vst[0:rows_in, r, :], ident[0:rows_in, 0:rows_in])
            t.then_inc(vec_turned, 1)
            def a_hi_products(k, slot, bank):
                w = whi[:, slot, k * P:(k + 1) * P]
                mm(ps[:, bank, 0:TM], w, xTA[:, k, 0:TM], start=(k == 0), stop=False)
                mm(ps[:, bank, 0:TM], w, xTA[:, k, TM:2 * TM], start=False, stop=False)

            pe.sem_inc(pe_taps, 2)
            pe.wait_ge(xn_ready, 3)
            pe.wait_ge(vec_ready, 1)
            pe.wait_ge(hi_ready, 1)
            for k in range(KT + 4):
                if k >= 4:
                    pe.wait_ge(xlo_ready, k - 3)
                    a_hi_products(k - 4, 0, 4)
                if k < KT:
                    b = ps[:, k % 4, :]
                    tr(b[:, 0:META], gB[0:META, k * P:(k + 1) * P], ident[0:META, 0:META])
                    for t in range(TOK):
                        i = tr(b[:, META + t * P:META + (t + 1) * P], tmp[:, t, k * P:(k + 1) * P], ident[:, :])
                    i.then_inc(turned, 1)

            def sums(first, count, bank, src):
                for k in range(count):
                    i = mm(ps[:, bank, 0:T], ones[:, :], src(first, k), start=False, stop=True, skip_group_check=True)
                return i

            def open_bank(bank, width=BANK):
                return mm(ps[:, bank, 0:width], zrow[:, 0:P], zrow[:, 0:width], start=True, stop=True)

            def a_group(g, first=False, sums=True):
                for s in range(4):
                    bank = 4 + s
                    if not first:
                        pe.wait_ge(glu_done, g * 2 + (s // 2 - 2 + 1 + 2))
                    if not (first and s == 0):
                        pe.wait_ge(hi_ready, g * 4 + (s + 1))
                        for k in range(KT):
                            a_hi_products(k, s % 2, bank)
                    pe.wait_ge(lo_pool, g * 4 + (s + 1))
                    for k in range(KT):
                        i = mm(ps[:, bank, 0:TM], wlo[:, s % 2, k * P:(k + 1) * P], xTA[:, k, 0:TM],
                               start=False, stop=(k == KT - 1))
                    i.then_inc(mm_done, 1)
                    if s == 1 and not first:
                        conv_taps(g, -1, PE_TAPS)
                if sums:
                    conv_sums(g, -4)

            def conv_taps(g, back, count):
                pe.wait_ge(glu_done, g * 2 + (2 * back + 2 + 2))
                if not (isinstance(g, int) and g + back == 0):
                    pe.wait_ge(conv_done, g * 2 + 2 * back)
                for m in range(2):
                    for q in range(count):
                        tap = TAPS - count + q
                        pe.wait_ge(diag_ready, g * (2 * PE_TAPS) + (2 * back * PE_TAPS + m * count + q + 1))
                        src = uext[:, ds(g * 2 + (2 * back + m), 1), tap:tap + T].rearrange("p a c -> p (a c)")
                        i = mm(ps[:, 2 + m, 0:T], diag[:, m * KT + q, :], src, start=(q == 0), stop=(q == count - 1))
                    i.then_inc(pe_taps, 1)

            def conv_sums(g, at):
                pe.wait_ge(conv_done, g * 2 + (at + 2))
                for m in range(2):
                    src = cv[:, ds(g * 2 + (at + m), 1), :].rearrange("p a c -> p (a c)")
                    i = mm(ps[:, 0, 0:T], ones[:, :], src, start=False, stop=True, skip_group_check=True)
                return i

            a_group(0, first=True, sums=False)
            a_group(1, sums=False)
            open_bank(0, T)
            open_bank(1, T)
            with pe.Fori(2, KT // 2) as g:
                a_group(g)
            conv_sums(KT // 2, -4)
            conv_taps(KT // 2, -1, PE_TAPS_LAST)
            conv_sums(KT // 2, -2).then_inc(sums_done, 1)
            pe.wait_ge(ws_in, 16)
            for hd in range(HEADS):
                t = tr(ps[:, 2 + hd // 4, (hd % 4) * P:(hd % 4 + 1) * P], wst[:, hd, :], ident[:, :])
            t.then_inc(ws_turned, 1)
            for q in range(4):
                pe.wait_ge(sq_done, q + 1)
                for k in range(4):
                    at = (q % 2) * 4 * T + k * T
                    i = mm(ps[:, 1, 0:T], ones[:, :], tmp[:, q // 2, at:at + T], start=False, stop=True, skip_group_check=True)
            i.then_inc(sums_done, 1)

            pe.wait_ge(gain_in, 16)
            pe.wait_ge(root_ready, 2)
            pe.wait_ge(glu_done, KT + 2)
            for t in range(TOK):
                for c in range(NC):
                    i = mm(ps[:, t * NC + c, :], ones[0:1, :], gB[0:1, c * BANK:(c + 1) * BANK], start=True, stop=True)
            i.then_inc(open_done, 1)

            def row_panel(n, s, step):
                pe.wait_ge(hi_ready, n + (s + 1))
                pe.wait_ge(act_hi, step)

                def all_banks(part, w):
                    for t in range(TOK):
                        for c in range(NC):
                            i = mm(ps[:, t * NC + c, :], act[:, s % 2, part, t * P:(t + 1) * P],
                                   w[:, s % 2, c * BANK:(c + 1) * BANK], start=False, stop=True, skip_group_check=True)
                    return i
                all_banks(0, whi)
                pe.wait_ge(act_lo, step)
                all_banks(1, whi)
                pe.wait_ge(lo_ready, n + (s + 1 - B))
                all_banks(0, wlo).then_inc(mm_done, 1)

            def last_row_panel(n, s, step):
                pe.wait_ge(hi_ready, n + (s + 1))
                pe.wait_ge(act_hi, step)
                pe.wait_ge(act_lo, step)
                for t in range(TOK):
                    for part, w in ((0, whi), (1, whi), (0, wlo)):
                        if w is wlo:
                            pe.wait_ge(lo_ready, n + (s + 1 - B))
                        for c in range(NC):
                            i = mm(ps[:, t * NC + c, :], act[:, s % 2, part, t * P:(t + 1) * P],
                                   w[:, s % 2, c * BANK:(c + 1) * BANK], start=False, stop=True, skip_group_check=True)
                    if t == 0:
                        i.then_inc(tok_done, 1)
                i.then_inc(mm_done, 1)

            def row_stage(n0, step, count):
                with pe.Fori(0, (count - 4) // 4) as r:
                    j = r * 4
                    for s in range(4):
                        row_panel(j + n0, s, j + (step + s + 1))
                for s in range(3):
                    row_panel(n0 + count - 4, s, step + count - 4 + s + 1)
                last_row_panel(n0 + count - 4, 3, step + count)

            row_stage(B, S_B, KT)

            def turn(count, bank):
                pe.wait_ge(xn_ready, 3 + 2 * count)
                for q in range(KT // 2):
                    if q >= 4:
                        pe.wait_ge(xlo_ready, KT * count + 2 * (q - 3))
                    for k in range(2):
                        for t in range(TOK):
                            at = (2 * q + k) * P
                            i = tr(ps[:, bank + q % 4, k * T + t * P:k * T + (t + 1) * P], tmp[:, t, at:at + P], ident[:, :])
                    i.then_inc(turned, 2)

            def feature_panel(n, s, f, bank, k0=0, count=KT, part=0, width=P, arrival=None):
                pe.wait_ge(feat_free, f)
                if part == 0:
                    pe.wait_ge(hi_ready, n + (s + 1))
                for k in range(count):
                    at = k * width + part * P
                    if arrival:
                        arrival(k0 + k)
                    mm(ps[:, bank, :], whi[:, s % 2, at:at + P], xT5[:, k0 + k, :], start=(k == 0), stop=False)
                if part == 0:
                    pe.wait_ge(lo_ready, n + (s + 1 - B))
                for k in range(count):
                    at = k * width + part * P
                    i = mm(ps[:, bank, 0:T], wlo[:, s % 2, at:at + P], xT5[:, k0 + k, 0:T],
                           start=False, stop=(k == count - 1))
                return i

            def feature_stage(n0, f0, count, arrival=None):
                peeled = 1 if arrival else 0
                for s in range(4 * peeled):
                    feature_panel(n0, s, f0 + s + 1, 4 + s, arrival=None if s else arrival).then_inc(mm_done, 1)
                with pe.Fori(peeled, (count) // 4) as r:
                    j = r * 4
                    for s in range(4):
                        feature_panel(j + n0, s, j + (f0 + s + 1), 4 + s).then_inc(mm_done, 1)

            turn(1, 0)
            feature_stage(C, F_C, 2 * FT, arrival=lambda k: pe.wait_ge(xlo_ready, KT + k + 1))
            pe.wait_ge(feat_free, F_E + 4)
            for b in range(8):
                open_bank(b)
            row_stage(DN, S_D, FT)
            turn(2, 4)

            for b in range(4):
                open_bank(b)
            for q in range(8):
                def banks(o, w):
                    for t in range(TOK):
                        for c in range(2):
                            for k in range(2):
                                i = mm(ps[:, 2 * t + c, :], xT5[:, 2 * q + k, o * T + t * P:o * T + (t + 1) * P],
                                       w[:, q % 2, k * SW + c * BANK:k * SW + (c + 1) * BANK],
                                       start=False, stop=True, skip_group_check=True)
                    return i
                pe.wait_ge(hi_ready, ZV + q + 1)
                pe.wait_ge(xlo_ready, 2 * KT + 2 * q + 2)
                banks(0, whi)
                banks(1, whi)
                pe.wait_ge(lo_ready, ZV + q + 1 - B)
                banks(0, wlo).then_inc(mm_done, 1)
            feature_stage(CH, F_E, 2 * CT)
            feature_stage(BG, F_E + BG - CH, CT)
            pe.wait_ge(ws_ready, 3)
            pe.wait_ge(v_ready, 2)
            pe.wait_ge(v_free, 4)
            for hd in range(HEADS):
                for t in range(TOK):
                    at = (hd % 2) * T + t * P
                    i = mm(ps[:, hd // 2, at:at + P], vbuf[:, t, hd * P:(hd + 1) * P], wsT[:, hd, :], start=True, stop=True)
            i.then_inc(spat_done, 1)
            feature_stage(U, F_E + U - CH, CT)
            feature_stage(GT, F_E + GT - CH, 2 * KT)
            def up_group(j, arrival=None):
                for s in range(4):
                    for b in range(2):
                        i = feature_panel(j + UP, s, j * 2 + (F_UP + 2 * s + b + 1), 4 + (2 * s + b) % 4,
                                          k0=(s % 2) * CT, count=CT, part=b, width=2 * P,
                                          arrival=arrival if s < 2 and b == 0 else None)
                    i.then_inc(mm_done, 1)

            up_group(0, arrival=lambda k: pe.wait_ge(pair_lo, k // 4 + 1))
            with pe.Fori(1, (2 * CT) // 4) as r:
                up_group(r * 4)
            pe.wait_ge(feat_free, F_END + 4)
            pe.wait_ge(vm_ready, 4)
            for b in range(8):
                open_bank(b)
            row_stage(G, S_G, KT)

            pe.wait_ge(xn_ready, 7 + 2)
            for q in range(8):
                for k in range(2):
                    for t in range(TOK):
                        i = tr(ps[:, q, k * T + t * P:k * T + (t + 1) * P], tmp[:, t, (2 * q + k) * P:(2 * q + k + 1) * P], ident[:, :])
                i.then_inc(tt_turned, 1)
            pe.wait_ge(tt_ready, 8)
            pe.wait_ge(wr_in, 32)
            pe.wait_ge(bias_in, 32)
            NL = GROUPS + EXPERTS
            for t in range(TOK):
                o = ps[:, 0, 32 * t:32 * t + NL]
                mm(o, ones[0:1, :], brow[0:1, :], start=True, stop=False)
                for k in range(KT):
                    i = mm(o, tiles[:, k, t * P:(t + 1) * P], wr[:, k, :], start=False, stop=(k == KT - 1))
            i.then_inc(logits_done, 1)
            pe.wait_ge(tri_ready, 1)
            pe.wait_ge(r_mask, 1)
            ohg = wk[:, OHG:OHG + 8]
            tri = wsT[:, 0, :]
            mm(ps[:, 1, 0:4], tri, ohg[:, 0:4], start=True, stop=True)
            mm(ps[:, 1, 4:8], ones[:, :], ohg[:, 0:4], start=True, stop=False)
            mm(ps[:, 1, 4:8], tri, ohg[:, 4:8], start=False, stop=True)
            mm(ps[:, 1, 8:12], ones[:, :], ohg[:, 0:4], start=True, stop=False)
            mm(ps[:, 1, 8:12], ones[:, :], ohg[:, 4:8], start=False, stop=True).then_inc(rank_done, 1)

            pe.wait_ge(tlo_ready, 2)
            gates = wk[:, GATE:GATE + 8]

            def gather(count, q):
                if not (isinstance(count, int) and count + q == 0):
                    pe.wait_ge(rows_ready, count + q)
                for t in range(TOK):
                    for src in (tH, tL):
                        i = mm(ps[:, 0, :], Sel[:, t, :], src[:, t, q * BANK:(q + 1) * BANK],
                               start=(t == 0 and src is tH), stop=(t == TOK - 1 and src is tL))
                i.then_inc(gath_done, 1)

            def turn_rows(count, q):
                pe.wait_ge(rows_ready, count + (q + 1))
                if q >= 2:
                    pe.wait_ge(xg_lo, count + q - 1)
                for k in range(4):
                    i = tr(ps[:, 3 - 2 * (q % 2), k * P:(k + 1) * P], tok_rows[:, (4 * q + k) * P:(4 * q + k + 1) * P], ident[:, :])
                i.then_inc(rows_turned, 1)

            def in_panel(n, s, q, bank):
                pe.wait_ge(hi_ready, n + (s + 1))
                for o in range(2):
                    for k in range(4):
                        mm(ps[:, bank, :], xg[:, o, 4 * q + k, :], whi[:, s % 2, k * DE:(k + 1) * DE],
                           start=(q == 0 and o == 0 and k == 0), stop=False)
                pe.wait_ge(lo_ready, n + (s + 1 - B))
                for k in range(4):
                    i = mm(ps[:, bank, :], xg[:, 0, 4 * q + k, :], wlo[:, s % 2, k * DE:(k + 1) * DE],
                           start=False, stop=(q == 3 and k == 3))
                i.then_inc(mm_done, 1)

            def expert_in(n, s0, bank):
                for q in range(4):
                    in_panel(n, s0 + q, q, bank)

            def down_panel(n, s, r, src):
                def banks(o, w):
                    for c in range(NC):
                        i = mm(ps[:, 4 + c, :], src[:, o, r, :], w[:, s % 2, c * BANK:(c + 1) * BANK],
                               start=False, stop=True, skip_group_check=True)
                    return i
                pe.wait_ge(hi_ready, n + (s + 1))
                banks(0, whi)
                banks(1, whi)
                pe.wait_ge(lo_ready, n + (s + 1 - B))
                banks(0, wlo).then_inc(mm_done, 1)

            def turn_hidden(count):
                pe.wait_ge(hid_e, count)
                for k in range(ET):
                    i = tr(ps[:, 2, k * P:(k + 1) * P], hid[:, k * P:(k + 1) * P], ident[:, :])
                i.then_inc(hid_turned, 1)

            def scatter(t, bank, chunks=range(NC)):
                for c in chunks:
                    mm(ps[:, bank + c, :], SelT[:, t, :], yh[:, 0, c * BANK:(c + 1) * BANK], start=True, stop=False)
                    mm(ps[:, bank + c, :], SelT[:, t, :], yh[:, 1, c * BANK:(c + 1) * BANK],
                       start=False, stop=True).then_inc(scat_done, 1)

            def scatter_first(jb, c):
                pe.wait_ge(y_lo, jb * 4 + (c + 1))
                scatter(0, 4, (c,))

            def scatter_second(jb, c):
                pe.wait_ge(add_done, jb * 8 + (24 + c + 1))
                scatter(1, 4, (c,))

            for b in range(4, 8):
                open_bank(b)
            pe.wait_ge(tri_ready, 3)
            pe.wait_ge(sel_ready, 2)
            gather(0, 0)
            for q in range(4):
                if q < 3:
                    gather(0, q + 1)
                turn_rows(0, q)
            pe.wait_ge(jobs_ready, 1)
            jobs = nc.tensor.value_load(sti[0:1, 0:1], min_val=GROUPS, max_val=GROUPS + 1)
            with pe.Fori(0, jobs) as jb:
                n = jb * JOB + MOE
                pe.wait_ge(xg_hi, jb * 4 + 4)
                pe.wait_ge(xg_lo, jb * 4 + 4)
                in_panel(n, 0, 0, 0)
                in_panel(n, 1, 1, 0)
                scatter_first(jb, 0)
                in_panel(n, 2, 2, 0)
                scatter_first(jb, 1)
                scatter_first(jb, 2)
                in_panel(n, 3, 3, 0)
                scatter_first(jb, 3)
                in_panel(n, 4, 0, 1)
                scatter_second(jb, 0)
                in_panel(n, 5, 1, 1)
                scatter_second(jb, 1)
                scatter_second(jb, 2)
                scatter_second(jb, 3)
                pe.wait_ge(gates_done, 1)
                for t in range(TOK):
                    tr(ps[:, 3, t * P:(t + 1) * P], Sel[:, t, :].bitcast(F32), ident[:, :])
                for t in range(TOK):
                    i = mm(ps[:, 3, 2 * P:2 * P + PER], Sel[:, t, :].bitcast(F32), gates[:, 4 * t:4 * t + 4],
                           start=(t == 0), stop=(t == TOK - 1))
                i.then_inc(slot_done, 1)
                in_panel(n, 6, 2, 1)
                in_panel(n, 7, 3, 1)

                def gate_up(n, s0, count):
                    pe.wait_ge(gsl_ready, count)
                    expert_in(n, s0, 0)
                    turn_hidden(count)
                    expert_in(n, s0 + 4, 1)

                pe.wait_ge(add_done, jb * 8 + (24 + 2 * NC))
                for b in range(4, 8):
                    open_bank(b)
                with pe.Fori(0, PER - 2) as e:
                    gate_up(n + e * 12, 8, jb * PER + e + 1)
                    pe.wait_ge(hT_lo, jb * PER + e + 1)
                    for r in range(ET):
                        down_panel(n + e * 12, 16 + r, r, hT)
                pe.wait_ge(gsl_ready, jb * PER + PER - 1)
                expert_in(n, JOB - 16, 0)
                turn_hidden(jb * PER + PER - 1)
                in_panel(n, JOB - 12, 0, 1)
                in_panel(n, JOB - 11, 1, 1)
                in_panel(n, JOB - 10, 2, 1)
                pe.wait_ge(gsl_ready, jb * PER + PER)
                pe.wait_ge(selT_ready, jb * 2 + 2)
                pe.wait_ge(sel_ready, jb * 2 + 4)
                gather(jb * 4 + 4, 0)
                in_panel(n, JOB - 9, 3, 1)
                gather(jb * 4 + 4, 1)
                pe.wait_ge(hT_lo, jb * PER + PER - 1)
                down_panel(n, JOB - 8, 0, hT)
                turn_rows(jb * 4 + 4, 0)
                gather(jb * 4 + 4, 2)
                down_panel(n, JOB - 7, 1, hT)
                turn_hidden(jb * PER + PER)
                turn_rows(jb * 4 + 4, 1)
                down_panel(n, JOB - 6, 2, hT)
                gather(jb * 4 + 4, 3)
                turn_rows(jb * 4 + 4, 2)
                down_panel(n, JOB - 5, 3, hT)
                pe.wait_ge(hT_lo, jb * PER + PER)
                down_panel(n, JOB - 4, 0, hT_last)
                turn_rows(jb * 4 + 4, 3)
                for r in range(1, ET):
                    down_panel(n, JOB - 4 + r, r, hT_last)
            pe.wait_ge(y_lo, jobs * 4 + 4)
            scatter(0, 4)
            pe.wait_ge(xg_lo, jobs * 4 + 4)
            scatter(1, 0)


_INS = ['x', 'meta_tokens', 'conv_w_in', 'conv_b_in', 'conv_w_dw', 'conv_b_dw', 'conv_ln_g', 'conv_ln_b',
        'conv_w_out', 'conv_b_out', 'norm_mix_pre', 'norm_mix_post', 'norm_ffn_pre', 'norm_ffn_post',
        'ffn_w_gate', 'ffn_w_up', 'ffn_w_down', 'norm_mix_g_2', 'w_in_2', 'conv_w_2', 'sgu_ln_g_2', 'sgu_ln_b_2',
        'sgu_w_s_2', 'sgu_b_s_2', 'w_up_conv_2', 'w_up_sgu_2', 'w_out_2', 'norm_ffn_g_2', 'w_router_group_2',
        'b_router_group_2', 'w_router_expert_2', 'b_router_expert_2', 'w_exp_gate_2', 'w_exp_up_2',
        'w_exp_down_2', 'norm_final_g_2']


def kernel(**inputs):
    import numpy as np
    import concourse.bacc as bacc
    from concourse.bass_utils import run_bass_kernel_spmd

    nc = bacc.Bacc("TRN2", target_bir_lowering=False, num_devices=1)
    arrays, args = {}, []
    for name in _INS:
        a = np.ascontiguousarray(inputs[name])
        arrays[f"in_{name}"] = a
        args.append(nc.dram_tensor(f"in_{name}", a.shape, mybir.dt.from_np(a.dtype), kind="ExternalInput").ap())
    o = nc.dram_tensor("out", inputs["x"].shape, F32, kind="ExternalOutput").ap()
    build_program(nc, *args, o)
    result = run_bass_kernel_spmd(nc, [arrays], core_ids=[0])
    return result.results[0]["out"]
```
